# Optimizing a Trainium2 kernel written in Bass

```python
import jax, jax.numpy as jnp
from jax import lax
import numpy as np

D_MODEL = 1024
BATCH = 1
SEQ = 1024
DEPTH = 2

N_META = 16
N_A_LAYERS = DEPTH // 2
N_B_LAYERS = DEPTH - N_A_LAYERS
LRU_WIDTH = D_MODEL
LRU_BLOCKS = 4
LRU_BLOCK = LRU_WIDTH // LRU_BLOCKS
CONV_WIDTH = 4
LRU_C = 8.0
ATTN_HEADS = 8
HEAD_DIM = 128
ATTN_WIDTH = ATTN_HEADS * HEAD_DIM
Q_BLOCK = 128
EPS = 1e-6

kernel_name = "yoco_hawk_fox_hybrid"

def rms_norm(x, g):
    xf = x.astype(jnp.float32)
    return xf * lax.rsqrt(jnp.mean(xf * xf, axis=-1, keepdims=True) + EPS) * g.astype(jnp.float32)

def causal_depthwise_conv(u, w, b):
    T = u.shape[1]
    up = jnp.pad(u, ((0, 0), (CONV_WIDTH - 1, 0), (0, 0)))
    out = b.astype(jnp.float32)
    for k in range(CONV_WIDTH):
        out = out + up[:, k:k + T] * w[k]
    return out

def block_diag_linear(u, w, b):
    B, T, _ = u.shape
    ub = u.reshape(B, T, LRU_BLOCKS, LRU_BLOCK)
    return jnp.einsum('btni,nij->btnj', ub, w).reshape(B, T, LRU_WIDTH) + b

def rg_lru(u, w_r, b_r, w_i, b_i, lam):
    r = jax.nn.sigmoid(block_diag_linear(u, w_r, b_r))
    i = jax.nn.sigmoid(block_diag_linear(u, w_i, b_i))
    log_a = -LRU_C * r * jax.nn.softplus(-lam.astype(jnp.float32))
    a = jnp.exp(log_a)
    mult = jnp.sqrt(-jnp.expm1(2.0 * log_a))
    bterm = mult * i * u

    def combine(left, right):
        a1, b1 = left
        a2, b2 = right
        return a1 * a2, a2 * b1 + b2

    _, h = lax.associative_scan(combine, (a, bterm), axis=1)
    return h

def recurrent_layer(x, g, w_in, conv_w, conv_b, w_r, b_r, w_i, b_i, lam, w_out):
    h = rms_norm(x, g)
    ug = h @ w_in
    u, gate = ug[..., :LRU_WIDTH], ug[..., LRU_WIDTH:]
    u = causal_depthwise_conv(u, conv_w, conv_b)
    y = rg_lru(u, w_r, b_r, w_i, b_i, lam)
    return (y * jax.nn.silu(gate)) @ w_out

def shared_kv(x, g_kv, w_kv, b_f, g_k):
    B, T, _ = x.shape
    h = rms_norm(x, g_kv)
    kvf = h @ w_kv
    k = kvf[..., :ATTN_WIDTH].reshape(B, T, ATTN_HEADS, HEAD_DIM)
    v = kvf[..., ATTN_WIDTH:2 * ATTN_WIDTH].reshape(B, T, ATTN_HEADS, HEAD_DIM)
    f_logit = kvf[..., 2 * ATTN_WIDTH:] + b_f
    k = rms_norm(k, g_k)
    cum = jnp.cumsum(jax.nn.log_sigmoid(f_logit.astype(jnp.float32)), axis=1)
    return (k.transpose(0, 2, 1, 3), v.astype(jnp.float32).transpose(0, 2, 1, 3), cum.transpose(0, 2, 1))

def forgetting_attention(q, k, v, cum):
    T = q.shape[2]
    scale = HEAD_DIM ** -0.5
    neg = jnp.finfo(jnp.float32).min
    bounds = [(0, N_META)] + [(s, min(s + Q_BLOCK, T)) for s in range(N_META, T, Q_BLOCK)]
    outs = []
    for s0, s1 in bounds:
        qb = q[:, :, s0:s1]
        kb = k[:, :, :s1]
        vb = v[:, :, :s1]
        logits = (jnp.einsum('bhqd,bhkd->bhqk', qb, kb) * scale
                  + cum[:, :, s0:s1, None] - cum[:, :, None, :s1])
        mask = jnp.arange(s0, s1)[:, None] >= jnp.arange(s1)[None, :]
        p = jax.nn.softmax(jnp.where(mask, logits, neg), axis=-1)
        outs.append(jnp.einsum('bhqk,bhkd->bhqd', p, vb))
    return jnp.concatenate(outs, axis=2)

def attention_layer(x, g, w_in, g_q, w_out, k, v, cum):
    B, T, _ = x.shape
    h = rms_norm(x, g)
    qg = h @ w_in
    q, gate = qg[..., :ATTN_WIDTH], qg[..., ATTN_WIDTH:]
    q = rms_norm(q.reshape(B, T, ATTN_HEADS, HEAD_DIM), g_q).transpose(0, 2, 1, 3)
    o = forgetting_attention(q, k, v, cum)
    o = o.transpose(0, 2, 1, 3).reshape(B, T, ATTN_WIDTH)
    return (o * jax.nn.silu(gate)) @ w_out

def setup_inputs(seed: int = 0) -> dict:
    key = jax.random.key(seed)
    ks = jax.random.split(key, 24)
    nA, nB = N_A_LAYERS, N_B_LAYERS
    f32 = jnp.float32

    def nrm(k, shape, scale):
        return jax.random.normal(k, shape, f32) * scale

    a8 = jax.random.uniform(ks[10], (nA, LRU_WIDTH), f32, 0.9, 0.999)
    a = a8 ** (1.0 / LRU_C)
    lam = jnp.log(a) - jnp.log1p(-a)
    b_f = jnp.linspace(1.0, 5.0, ATTN_HEADS, dtype=f32) + nrm(ks[14], (ATTN_HEADS,), 0.1)
    return {
        "x": nrm(ks[0], (BATCH, SEQ, D_MODEL), 1.0),
        "meta_tokens": nrm(ks[1], (N_META, D_MODEL), 1.0),
        "a_norm": 1.0 + nrm(ks[2], (nA, D_MODEL), 0.02),
        "a_w_in": nrm(ks[3], (nA, D_MODEL, 2 * LRU_WIDTH), D_MODEL ** -0.5),
        "a_conv_w": nrm(ks[4], (nA, CONV_WIDTH, LRU_WIDTH), CONV_WIDTH ** -0.5),
        "a_conv_b": nrm(ks[5], (nA, LRU_WIDTH), 0.01),
        "a_w_r": nrm(ks[6], (nA, LRU_BLOCKS, LRU_BLOCK, LRU_BLOCK), LRU_BLOCK ** -0.5),
        "a_b_r": nrm(ks[7], (nA, LRU_WIDTH), 0.01),
        "a_w_i": nrm(ks[8], (nA, LRU_BLOCKS, LRU_BLOCK, LRU_BLOCK), LRU_BLOCK ** -0.5),
        "a_b_i": nrm(ks[9], (nA, LRU_WIDTH), 0.01),
        "a_lambda": lam,
        "a_w_out": nrm(ks[11], (nA, LRU_WIDTH, D_MODEL), LRU_WIDTH ** -0.5),
        "kv_norm": 1.0 + nrm(ks[12], (D_MODEL,), 0.02),
        "w_kv": nrm(ks[13], (D_MODEL, 2 * ATTN_WIDTH + ATTN_HEADS), D_MODEL ** -0.5),
        "b_f": b_f,
        "k_norm": 1.0 + nrm(ks[15], (HEAD_DIM,), 0.02),
        "b_norm": 1.0 + nrm(ks[16], (nB, D_MODEL), 0.02),
        "b_w_in": nrm(ks[17], (nB, D_MODEL, 2 * ATTN_WIDTH), D_MODEL ** -0.5),
        "q_norm": 1.0 + nrm(ks[18], (nB, HEAD_DIM), 0.02),
        "b_w_out": nrm(ks[19], (nB, ATTN_WIDTH, D_MODEL), ATTN_WIDTH ** -0.5),
    }

def reference(x, meta_tokens, a_norm, a_w_in, a_conv_w, a_conv_b, a_w_r, a_b_r, a_w_i, a_b_i,
              a_lambda, a_w_out, kv_norm, w_kv, b_f, k_norm, b_norm, b_w_in, q_norm, b_w_out):
    B = x.shape[0]
    meta = jnp.broadcast_to(meta_tokens[None].astype(x.dtype), (B, N_META, D_MODEL))
    h = jnp.concatenate([meta, x], axis=1)
    k = v = cum = None
    for l in range(DEPTH):
        if l < N_A_LAYERS:
            out = recurrent_layer(h, a_norm[l], a_w_in[l], a_conv_w[l], a_conv_b[l], a_w_r[l],
                                  a_b_r[l], a_w_i[l], a_b_i[l], a_lambda[l], a_w_out[l])
        else:
            if l == N_A_LAYERS:
                k, v, cum = shared_kv(h, kv_norm, w_kv, b_f, k_norm)
            j = l - N_A_LAYERS
            out = attention_layer(h, b_norm[j], b_w_in[j], q_norm[j], b_w_out[j], k, v, cum)
        h = h + out.astype(h.dtype)
    return h[:, N_META:]


_drawn_inputs = setup_inputs


def setup_inputs(seed=0):
    import zlib

    import numpy as np

    out = dict(_drawn_inputs(seed))
    spreads = {}
    factors = {'a_norm': 5.574,
     'a_b_r': 8.0,
     'a_b_i': 8.0,
     'kv_norm': 8.0,
     'k_norm': 8.0,
     'b_norm': 8.0,
     'q_norm': 8.0}
    for name, (base, spread) in spreads.items():
        noise = np.random.default_rng([zlib.crc32(name.encode()), seed]).standard_normal(out[name].shape)
        drawn = base * np.exp(spread * noise) if base else spread * noise
        out[name] = __import__('jax').numpy.asarray(drawn.astype(out[name].dtype))
    for name, factor in factors.items():
        out[name] = (out[name] * factor).astype(out[name].dtype)
    return out
```

```python
from contextlib import ExitStack

import concourse.bass as bass
from concourse import mybir

F32 = mybir.dt.float32
F32R = mybir.dt.float32r
BF16 = mybir.dt.bfloat16
ALU = mybir.AluOpType
ACT = mybir.ActivationFunctionType

P = 128
D = 1024
C = D // P
META = 16
SEQ = 1024
T = META + SEQ
HEADS = 8
QB = SEQ // P
TAPS = 4
LRU_BLOCKS = 4
EPS = 1e-6
LO_CUT = 400
MASKED = -1e30
BANK = 512

ALL_TOKENS = [(0, 346), (346, 346), (692, 348)]
REAL_TOKENS = [(META, 342), (META + 342, 342), (META + 684, 340)]

PER_ROUND = {"A": 6, "Y": 2, "B": 4, "O": 2}
FIRST_JOB = {"A": 0, "Y": 6 * LRU_BLOCKS, "B": 6 * LRU_BLOCKS + C, "O": 6 * LRU_BLOCKS + C + 4 * HEADS}
W_PER_ROUND = {"A": 4, "Y": 2, "B": 4, "O": 2}
W_FIRST = {"A": 0, "Y": 4 * LRU_BLOCKS, "B": 4 * LRU_BLOCKS + C, "O": 4 * LRU_BLOCKS + C + 4 * HEADS}
ROUNDS_OUT = C // 2

V_A_NORM, V_KV_NORM, V_B_NORM = 0, C, 2 * C
V_CONV_W = 3 * C
V_CONV_B = V_CONV_W + TAPS * C
V_B_R, V_B_I, V_LAMBDA = V_CONV_B + C, V_CONV_B + 2 * C, V_CONV_B + 3 * C
V_K_NORM = V_LAMBDA + C
V_Q_NORM = V_K_NORM + 1
V_B_F = V_Q_NORM + 1
V_ALL = V_B_F + 1
V_KQ = V_ALL
V_T = V_KQ + 1
V_E = V_T + C
V_S = V_E + C
V_END = V_S + 5 * C
VEC_STEPS = 22

WIDTH = [META + P * (i + 1) for i in range(QB)]
ROW = [sum(WIDTH[:i]) for i in range(QB)]
ROWS = sum(WIDTH)


def pieces_of(width):
    n = -(-width // BANK)
    step = width // n // 2 * 2
    return [(a * step, step if a < n - 1 else width - step * (n - 1)) for a in range(n)]


PIECES = [(i, a, n, a + n == WIDTH[i]) for i in range(QB) for a, n in pieces_of(WIDTH[i])]
NP = len(PIECES)
LAST_PIECE = [max(s for s, p in enumerate(PIECES) if p[0] == i) for i in range(QB)]
FIRST_PIECE = [min(s for s, p in enumerate(PIECES) if p[0] == i) for i in range(QB)]

UNITS = [(j, c, max(0, c - 1 - 4 * j)) for j in range(2) for c in range(0, 4 * j + 5)]
NU = len(UNITS)
TILE_END = [max(u for u, x in enumerate(UNITS) if x[0] == j) for j in range(2)]
V_UNITS = [(0, 1), (1, 4), (4, 7), (7, 9)]
NV = len(V_UNITS)
VALUES_AT = [(0, 1), (2,), (3,)]
OG_AT = [0, 1, 3, 5, 7, 9, 11]
UNIT_WITH_Q = 1
OUT_CHUNK_AT = [3, 5, 7, 8, 9, 11, 12]


GATE_STEPS = [(t, c) for t in range(3) for c in range(C)]
GATE_IN_UNITS = len(GATE_STEPS) - NP
TILE_1_PIECE = 2 * C - 1 - GATE_IN_UNITS
ROW_WITH_TILE_1 = min(i for i in range(QB) if LAST_PIECE[i] > TILE_1_PIECE)


def key_at(c):
    return 0 if c == 0 else META + P * (c - 1)


def after(eng, sem, value):
    if isinstance(value, int) and value <= 0:
        return
    eng.wait_ge(sem, value)


def part(tensor, index, size=T):
    return tensor[:, bass.ds(index * size, size)]


def job_of(phase, i, k):
    return FIRST_JOB[phase] + PER_ROUND[phase] * i + k


def trunk(nc, x_t, vectors, w_jobs, w_ri, w_f, out_t, x1_dram, ncum_dram):
    with ExitStack() as ctx:
        def sem(name):
            return ctx.enter_context(nc.semaphore(name))

        base = (nc.sbuf_base + 63) // 64 * 64
        top = [base]

        def put(name, cols, dt=F32, parts=P, at=None):
            size = cols * (2 if dt == BF16 else 4)
            where = top[0] if at is None else at[0]
            t = nc.alloc_sbuf_tensor_at(name, [parts, cols], dt, offset=where)
            (top if at is None else at)[0] = (where + size + 31) // 32 * 32
            return t

        h_hi, h_lo = put("h_hi", C * T, F32R), put("h_lo", C * T, F32R)
        w_raw = [put(f"w_raw{i}", D) for i in range(2)]
        w_hi = [put(f"w_hi{i}", D, F32R) for i in range(2)]
        w_lo = [put(f"w_lo{i}", D, F32R) for i in range(2)]
        vec = put("vec", V_END)
        ident = put("ident", P)
        eps = put("eps", 1)
        idle_act, idle_dve, idle_pool = put("idle_act", 12), put("idle_dve", NP), put("idle_pool", QB)
        ident_bf, causal_bf = put("ident_bf", P, BF16), put("causal_bf", P, BF16)
        ones = put("ones", P)
        wf_raw = put("wf_raw", C * HEADS)
        shift, total, inv_total = put("shift", NP), put("total", QB), put("inv_total", QB)
        region_y = top[0]
        y_hi, y_lo = put("y_hi", C * T, F32R), put("y_lo", C * T, F32R)
        scratch = top[0]

        x_raw = put("x_raw", C * T, at=[region_y])
        at = [scratch]
        u_in = put("u_in", 4 + T, at=at)
        u_conv = [put(f"u_conv{k}", T, at=at) for k in range(2)]
        uc_hi = [put(f"uc_hi{k}", T, F32R, at=at) for k in range(2)]
        uc_lo = [put(f"uc_lo{k}", T, F32R, at=at) for k in range(2)]
        gate = [put(f"gate{k}", T, at=at) for k in range(2)]
        r_buf, i_buf, a_buf = (put(n, T, at=at) for n in ("r_buf", "i_buf", "a_buf"))
        end = at[0]
        at = [scratch]
        x1 = put("x1", C * T, at=at)
        tmp = [put(f"tmp{i}", T, at=at) for i in range(2)]
        sq, acc = put("sq", T, at=at), put("acc", T, at=at)
        end = max(end, at[0])
        at = [scratch]
        og = put("og", HEADS * SEQ, at=at)
        prob = put("prob", ROWS, at=at)
        end = max(end, at[0])
        at = [region_y]
        k_hi, k_lo = put("k_hi", T, F32R, at=at), put("k_lo", T, F32R, at=at)
        q_hi, q_lo = put("q_hi", T, F32R, at=at), put("q_lo", T, F32R, at=at)
        v_hi, v_lo = put("v_hi", 9 * P, F32R, at=at), put("v_lo", 9 * P, F32R, at=at)
        k_raw = put("k_raw", T, at=at)
        decay = k_raw
        q_raw, v_raw = put("q_raw", T, at=at), put("v_raw", T, at=at)
        pt_hi = [put(f"pt_hi{i}", BANK, F32R, at=at) for i in range(2)]
        pt_lo = [put(f"pt_lo{i}", BANK, F32R, at=at) for i in range(2)]
        square = put("square", T, at=at)
        ms = put("ms", T, at=at)
        rs = put("rs", T, at=at)
        assert at[0] <= scratch and end <= nc.sbuf_usable_end, (at[0], scratch, end)
        at = [region_y]
        wf_hi, wf_lo = put("wf_hi", C * P, F32R, at=at), put("wf_lo", C * P, F32R, at=at)
        at = [region_y]
        x1_in = [put(f"x1_in{i}", SEQ, at=at) for i in range(2)]
        y_out = [put(f"y_out{i}", SEQ, at=at) for i in range(2)]

        pj = [ctx.enter_context(nc.psum_tensor(f"pj{t}", [P, BANK], F32)) for t in range(3)]
        ps = [ctx.enter_context(nc.psum_tensor(f"ps{t}", [P, BANK], F32)) for t in range(2)]
        pt = [ctx.enter_context(nc.psum_tensor(f"pt{t}", [P, BANK], F32)) for t in range(2)]
        po = ctx.enter_context(nc.psum_tensor("po", [P, BANK], F32))
        p_i = [ps[0], ps[1], pt[0]]

        def sems(*names):
            return [sem(n) for n in names]

        vec_in, wf_in, x_in, w_in = sem("vec_in"), sem("wf_in"), sems(*(f"x_in{c}" for c in range(C))), sems("w_in0", "w_in1")
        const_set, ident_zero, ident_set, vec_step, wf_scaled, wf_zero, wf_hi_set, wf_lo_set = sems(
            "const_set", "ident_zero", "ident_set", "vec_step", "wf_scaled", "wf_zero", "wf_hi_set", "wf_lo_set")
        w_scaled = {"A": sem("w_scaled_a"), "B": sem("w_scaled_b")}
        w_hi_set, w_split = sems("w_hi_set", "w_split")
        norms = [{k: sem(f"norm{i}_{k}") for k in ("zero", "sq", "acc", "sum", "ms", "rs0", "rs", "h", "hi",
                                                    "lo_pool", "lo_dve")} for i in range(2)]
        a_proj, pad_set, u_set, conv_step, conv_done, uc_hi_set, uc_lo_set = sems(
            "a_proj", "pad_set", "u_set", "conv_step", "conv_done", "uc_hi_set", "uc_lo_set")
        gate_tanh, gate_set, ri_set, a_set, t_set, mult_set, m_step, y_set, y_hi_set, y_lo_set = sems(
            "gate_tanh", "gate_set", "ri_set", "a_set", "t_set", "mult_set", "m_step", "y_set", "y_hi_set",
            "y_lo_set")
        ao_proj, x_back, x1_set, x1_out = sem("ao_proj"), sems("x_back0", "x_back1"), sem("x1_set"), sem("x1_out")
        f_proj, f_in, f_step, f_ln, f_ls, f_cum, f_ones, ncum_out = sems(
            "f_proj", "f_in", "f_step", "f_ln", "f_ls", "f_cum", "f_ones", "ncum_out")
        b_proj, kqv_in, stat_sum, ms_set, rs0_set, newton, kq_scaled, kq_hi_set, kq_lo_set = sems(
            "b_proj", "kqv_in", "stat_sum", "ms_set", "rs0_set", "newton", "kq_scaled", "kq_hi_set", "kq_lo_set")
        decay_in, scores, logits, row_exp, inv_set, row_norm, gate2_tanh, gate2_set = sems(
            "decay_in", "scores", "logits", "row_exp", "inv_set", "row_norm", "gate2_tanh", "gate2_set")
        turned, turned_hi, turned_lo, pv_done, og_set, v_zero = sems(
            "turned", "turned_hi", "turned_lo", "pv_done", "og_set", "v_zero")
        og_hi_set, og_lo_pool, og_lo_dve, o_proj, y_added = sems(
            "og_hi_set", "og_lo_pool", "og_lo_dve", "o_proj", "y_added")
        x1_back, y_stored = sems("x1_back0", "x1_back1"), sems("y_stored0", "y_stored1")

        def col(offset, index=0, parts=P):
            return vec[0:parts, bass.ds(offset + index, 1)]

        def weights_in(phase, i, k):
            return 16 * ((FIRST_JOB[phase] + k) // 2 + PER_ROUND[phase] // 2 * i + 1)

        def width_of(phase, k):
            return 4 * P if phase == "A" and k >= 4 else D

        block = ctx.enter_context(nc.Block())

        @block.sync
        def _(sp):
            def load(phase, i, k):
                after(sp, w_split, job_of(phase, i, k) - 1)
                if phase == "A" and k >= 4:
                    source = w_ri[bass.ds(2 * i + k - 4, 1)]
                else:
                    source = w_jobs[bass.ds(W_FIRST[phase] + W_PER_ROUND[phase] * i + k, 1)]
                sp.dma_start(w_raw[k % 2][:, 0:width_of(phase, k)],
                             source.rearrange("a p n -> (a p) n")).then_inc(w_in[k % 2], 16)

            sp.dma_start(vec[:, 0:V_ALL], vectors).then_inc(vec_in, 16)
            sp.dma_start(wf_raw[:], w_f).then_inc(wf_in, 16)
            for c in range(C):
                sp.dma_start(part(x_raw, c), x_t[c]).then_inc(x_in[c], 16)
                if c == 1:
                    load("A", 0, 0)
            for k in range(1, 6):
                load("A", 0, k)
            with sp.Fori(1, LRU_BLOCKS) as n:
                for k in range(6):
                    load("A", n, k)

            def chunk_again(m, k):
                after(sp, x1_set, 3 * (2 * m + k) - 3)
                sp.dma_start(tmp[k][:], x_t[bass.ds(2 * m + k, 1)].rearrange("a p n -> (a p) n")).then_inc(x_back[k], 16)

            load("Y", 0, 0)
            load("Y", 0, 1)
            sp.wait_ge(y_lo_set, C)
            chunk_again(0, 0)
            chunk_again(0, 1)
            with sp.Fori(1, ROUNDS_OUT) as m:
                for k in range(2):
                    load("Y", m, k)
                    chunk_again(m, k)
            load("B", 0, 0)
            load("B", 0, 1)
            sp.wait_ge(x1_set, 3 * C)
            sp.dma_start(x1_dram, x1[:].rearrange("p (c t) -> p c t", c=C)).then_inc(x1_out, 16)

            def rest_of_round(h, first):
                for k in range(first, 4):
                    load("B", h, k)
                sp.wait_ge(kq_lo_set, 2 * h + 1)
                sp.dma_start(decay[:], ncum_dram[bass.ds(h, 1), :].to_broadcast([P, T])).then_inc(decay_in, 16)

            sp.wait_ge(f_cum, 1)
            sp.dma_start(ncum_dram, v_raw[0:HEADS, :]).then_inc(ncum_out, 16)
            sp.wait_ge(ncum_out, 16)
            rest_of_round(0, 2)
            with sp.Fori(1, HEADS) as h:
                rest_of_round(h, 0)

            def x1_again(m, k):
                after(sp, y_added, 3 * (2 * m + k) - 3)
                sp.dma_start(x1_in[k][:], x1_dram[:, bass.ds(2 * m + k, 1), META:T].rearrange("p a t -> p (a t)")
                             ).then_inc(x1_back[k], 16)

            load("O", 0, 0)
            load("O", 0, 1)
            sp.wait_ge(x1_out, 16)
            sp.wait_ge(scores, NP * HEADS)
            x1_again(0, 0)
            x1_again(0, 1)
            with sp.Fori(1, ROUNDS_OUT) as m:
                for k in range(2):
                    load("O", m, k)
                    x1_again(m, k)
            for k in range(2):
                sp.wait_ge(y_stored[k], 16 * ROUNDS_OUT)

        @block.tensor
        def _(pe):
            def product(out, pairs):
                for i, ((a_hi, a_lo), (b_hi, b_lo)) in enumerate(pairs):
                    pe.matmul(out, a_hi, b_hi, start=(i == 0), stop=False)
                    pe.matmul(out, a_hi, b_lo, start=False, stop=False)
                    last = pe.matmul(out, a_lo, b_hi, start=False, stop=(i == len(pairs) - 1))
                return last

            def w_chunk(slot, c):
                return w_hi[slot][:, c * P:(c + 1) * P], w_lo[slot][:, c * P:(c + 1) * P]

            def moving(hi, lo, c, a, n):
                return hi[:, c * T + a:c * T + a + n], lo[:, c * T + a:c * T + a + n]

            def project(slot, t, tiles, hi, lo, shift=0):
                a, n = tiles[t]
                return product(pj[t][:, 0:n], [(w_chunk(slot, c), moving(hi, lo, c, a - shift, n)) for c in range(C)])

            def project_as_chunks_come(weights, tiles, ready, done, shift=0):
                for c in range(C):
                    for s in ready:
                        pe.wait_ge(s, c + 1)
                    for t, (a, n) in enumerate(tiles):
                        (wh, wl), (xh, xl) = weights(c), moving(h_hi, h_lo, c, a - shift, n)
                        pe.matmul(pj[t][:, 0:n], wh, xh, start=(c == 0), stop=False)
                        pe.matmul(pj[t][:, 0:n], wh, xl, start=False, stop=False)
                        m = pe.matmul(pj[t][:, 0:n], wl, xh, start=False, stop=(c == C - 1))
                        if c == C - 1:
                            m.then_inc(done, 1)

            def norm_sums(norm):
                pe.wait_ge(norm["acc"], C)
                for t, (a, n) in enumerate(ALL_TOKENS):
                    pe.matmul(pj[t][:, 0:n], ones[:], acc[:, a:a + n], start=True, stop=True).then_inc(norm["sum"], 1)

            pe.wait_ge(const_set, 1)
            norm_sums(norms[0])

            def layer_a(n, peeled=False):
                for k in range(4):
                    pe.wait_ge(w_split, 6 * n + k + 1)
                    if k == 0 and peeled:
                        pe.wait_ge(norms[0]["ms"], 3)
                        project_as_chunks_come(lambda c: w_chunk(0, c), ALL_TOKENS,
                                               (norms[0]["lo_pool"], norms[0]["lo_dve"]), a_proj)
                        continue
                    for t in range(3):
                        if k == 0:
                            pe.wait_ge(ri_set, 12 * n - 5 + t)
                        elif k < 3:
                            pe.wait_ge(u_set, 6 * n + 3 * (k - 1) + 1 + t)
                        else:
                            pe.wait_ge(gate_set, 6 * n + 1 + t)
                        project(k % 2, t, ALL_TOKENS, h_hi, h_lo).then_inc(a_proj, 1)
                pe.wait_ge(uc_lo_set, 2 * n + 2)
                for k in range(2):
                    pe.wait_ge(w_split, 6 * n + 5 + k)
                    for g in range(2):
                        for t, (a, m) in enumerate(ALL_TOKENS):
                            if g == 0 and k == 0:
                                pe.wait_ge(gate_set, 6 * n + 4 + t)
                            elif g == 0:
                                pe.wait_ge(ri_set, 12 * n + 1 + t)
                            else:
                                after(pe, ri_set, 12 * n - 2 + 6 * k + t)
                            product((pj, p_i)[g][t][:, 0:m], [
                                (w_chunk(k, 2 * g + c), (uc_hi[c][:, a:a + m], uc_lo[c][:, a:a + m]))
                                for c in range(2)]).then_inc(a_proj, 1)

            layer_a(0, peeled=True)
            with pe.Fori(1, LRU_BLOCKS) as n:
                layer_a(n)

            def layer_a_out(m, peeled=False):
                for k in range(2):
                    pe.wait_ge(w_split, FIRST_JOB["Y"] + 2 * m + k + 1)
                    for t in range(3):
                        if peeled and k == 0:
                            pe.wait_ge(ri_set, 12 * LRU_BLOCKS - 5 + t)
                        else:
                            pe.wait_ge(x1_set, 3 * (2 * m + k) - 2 + t)
                        project(k, t, ALL_TOKENS, y_hi, y_lo).then_inc(ao_proj, 1)

            pe.wait_ge(y_lo_set, C)
            layer_a_out(0, peeled=True)
            with pe.Fori(1, ROUNDS_OUT) as m:
                layer_a_out(m)

            pe.wait_ge(x1_set, 3 * C)
            norm_sums(norms[1])
            pe.wait_ge(wf_lo_set, 1)
            pe.wait_ge(norms[1]["ms"], 3)
            project_as_chunks_come(lambda c: (wf_hi[:, c * P:(c + 1) * P], wf_lo[:, c * P:(c + 1) * P]),
                                   ALL_TOKENS, (norms[1]["lo_pool"], norms[1]["lo_dve"]), f_proj)

            def head_squares(h, which):
                for t, (a, n) in enumerate(ALL_TOKENS):
                    if which == 0 and t == 0:
                        after(pe, logits, NP * h)
                    elif which == 1 or t == 2:
                        pe.wait_ge(ms_set, 6 * h + 3 * which + t - 1)
                    pe.wait_ge(kqv_in, 9 * h + 3 * which + t + 1)
                    pe.matmul(ps[(t + which) % 2][:, 0:n], ones[:], square[:, a:a + n],
                              start=True, stop=True).then_inc(stat_sum, 1)

            def gate_steps(h, first, end):
                for t, c in GATE_STEPS[first:end]:
                    a, n = REAL_TOKENS[t]
                    (wh, wl), (xh, xl) = w_chunk(1, c), moving(h_hi, h_lo, c, a, n)
                    if c == 0:
                        pe.wait_ge(kqv_in, 9 * h + 7 + t)
                    pe.matmul(pj[t][:, 0:n], wh, xh, start=(c == 0), stop=False)
                    pe.matmul(pj[t][:, 0:n], wh, xl, start=False, stop=False)
                    m = pe.matmul(pj[t][:, 0:n], wl, xh, start=False, stop=(c == C - 1))
                    if c == C - 1:
                        m.then_inc(b_proj, 1)

            def probs_times_values(h, between):
                before = 18 * h + NV
                pe.wait_ge(turned_lo, before)

                def turn(u):
                    j, c, b0 = UNITS[u]
                    pe.wait_ge(turned_lo, before + u - 1)
                    if c == 0:
                        pe.wait_ge(row_norm, QB * h + 4 * (j + 1))
                    for b in range(b0, 4):
                        at = ROW[4 * j + b] + key_at(c)
                        m = pe.transpose(pt[u % 2][:, b * P:(b + 1) * P], prob[:, at:at + P], ident[:])
                    m.then_inc(turned, 1)

                def multiply(u):
                    j, c, b0 = UNITS[u]
                    pe.wait_ge(turned_lo, before + u + 1)
                    if c == 0 and j == 1:
                        pe.wait_ge(og_set, 2 * h + 1)
                    a = b0 * P
                    vh, vl = (v[:, c * P:(c + 1) * P] for v in (v_hi, v_lo))
                    ph, pl = (p[u % 2][:, a:BANK] for p in (pt_hi, pt_lo))
                    pe.matmul(po[:, a:BANK], vh, ph, start=(c == 0), stop=False)
                    pe.matmul(po[:, a:BANK], vh, pl, start=False, stop=False)
                    pe.matmul(po[:, a:BANK], vl, ph, start=False, stop=(u == TILE_END[j])).then_inc(pv_done, 1)

                turn(0)
                for u in range(NU):
                    if u + 1 < NU:
                        turn(u + 1)
                    between(u)
                    multiply(u)

            def all_scores(h):
                pe.wait_ge(kq_lo_set, 2 * h + 2)
                for s, (i, a, n, diagonal) in enumerate(PIECES):
                    if s < 2:
                        pe.wait_ge(ms_set, 6 * h + 6)
                    else:
                        pe.wait_ge(logits, NP * h + s - 1)
                    rows, keys = slice(META + P * i, META + P * (i + 1)), slice(a, a + n)
                    bank = ps[s % 2]
                    pe.matmul(bank[:, 0:n], q_hi[:, rows], k_hi[:, keys], start=True, stop=False)
                    pe.matmul(bank[:, 0:n], q_hi[:, rows], k_lo[:, keys], start=False, stop=False)
                    m = pe.matmul(bank[:, 0:n], q_lo[:, rows], k_hi[:, keys], start=False, stop=not diagonal)
                    if diagonal:
                        m = pe.matmul(bank[:, n - P:n], ident_bf[:], causal_bf[:], start=False, stop=True)
                    m.then_inc(scores, 1)
                    gate_steps(h, GATE_IN_UNITS + s, GATE_IN_UNITS + s + 1)

            def turn_values(h, units):
                for v in units:
                    c0, c1 = V_UNITS[v]
                    if v < 2:
                        pe.wait_ge(kqv_in, 9 * h + 9)
                    else:
                        pe.wait_ge(turned_lo, 18 * h + v - 1)
                    for c in range(c0, c1):
                        m = pe.transpose(pt[v % 2][:, (c - c0) * P:(c - c0 + 1) * P],
                                         v_raw[:, key_at(c):key_at(c) + P], ident[:])
                    m.then_inc(turned, 1)

            def layer_b(h, peeled=False):
                for k, tiles in ((0, ALL_TOKENS), (1, REAL_TOKENS), (2, ALL_TOKENS)):
                    pe.wait_ge(w_split, FIRST_JOB["B"] + 4 * h + k + 1)
                    for t in range(3):
                        if k == 0 and peeled:
                            pe.wait_ge(f_in, t + 1)
                        elif k == 0:
                            pe.wait_ge(gate2_set, 3 * h - 2 + t)
                        else:
                            pe.wait_ge(kqv_in, 9 * h + 3 * (k - 1) + t + 1)
                        project(k % 2, t, tiles, h_hi, h_lo).then_inc(b_proj, 1)
                        if k == 0 and not peeled:
                            turn_values(h - 1, VALUES_AT[t])
                        if k > 0 and t == 0:
                            head_squares(h, k - 1)
                pe.wait_ge(w_split, FIRST_JOB["B"] + 4 * h + 4)
                if peeled:
                    gate_steps(h, 0, GATE_IN_UNITS)
                else:
                    probs_times_values(h - 1, lambda u: gate_steps(
                        h, u * GATE_IN_UNITS // NU, (u + 1) * GATE_IN_UNITS // NU))
                all_scores(h)

            layer_b(0, peeled=True)
            with pe.Fori(1, HEADS) as h:
                layer_b(h)

            def first_out_chunk(c):
                pe.wait_ge(og_lo_pool, c + 1)
                pe.wait_ge(og_lo_dve, c + 1)
                for t, (a, n) in enumerate(REAL_TOKENS):
                    (wh, wl), (xh, xl) = w_chunk(0, c), moving(h_hi, h_lo, c, a - META, n)
                    pe.matmul(pj[t][:, 0:n], wh, xh, start=(c == 0), stop=False)
                    pe.matmul(pj[t][:, 0:n], wh, xl, start=False, stop=False)
                    m = pe.matmul(pj[t][:, 0:n], wl, xh, start=False, stop=(c == C - 1))
                    if c == C - 1:
                        m.then_inc(o_proj, 1)

            def out_chunks_between(u):
                if u in OUT_CHUNK_AT:
                    first_out_chunk(OUT_CHUNK_AT.index(u))

            turn_values(HEADS - 1, range(NV))
            pe.wait_ge(w_split, FIRST_JOB["O"] + 1)
            pe.wait_ge(gate2_set, 3 * HEADS)
            probs_times_values(HEADS - 1, out_chunks_between)
            first_out_chunk(HEADS - 1)

            def layer_b_out(m, first=0):
                for k in range(first, 2):
                    pe.wait_ge(w_split, FIRST_JOB["O"] + 2 * m + k + 1)
                    for t in range(3):
                        pe.wait_ge(y_added, 3 * (2 * m + k) - 2 + t)
                        project(k, t, REAL_TOKENS, h_hi, h_lo, META).then_inc(o_proj, 1)

            layer_b_out(0, first=1)
            with pe.Fori(1, ROUNDS_OUT) as m:
                layer_b_out(m)

        @block.scalar
        def _(act):
            def round_weights(phase, i, k):
                if phase in w_scaled and k < 4:
                    act.wait_ge(w_scaled[phase], 4 * i + k + 1)
                else:
                    act.wait_ge(w_in[k % 2], weights_in(phase, i, k))
                cols = slice(0, width_of(phase, k))
                act.activation(w_hi[k % 2][:, cols], w_raw[k % 2][:, cols], ACT.Identity).then_inc(w_hi_set, 1)

            def square_chunk(norm, source, c):
                after(act, norm["acc"], c)
                act.activation(sq[:], part(source, c), ACT.Square).then_inc(norm["sq"], 1)

            def inverse_root(norm):
                for t, (a, n) in enumerate(ALL_TOKENS):
                    act.wait_ge(norm["sum"], t + 1)
                    act.activation(sq[:, a:a + n], pj[t][:, 0:n], ACT.Identity, scale=1.0 / D,
                                   bias=eps[:]).then_inc(norm["ms"], 1)
                act.wait_ge(norm["ms"], 3)
                act.activation(acc[:], sq[:], ACT.Ln).then_inc(norm["rs0"], 1)
                act.wait_ge(norm["rs0"], 1)
                act.activation(acc[:], acc[:], ACT.Exp, scale=-0.5).then_inc(norm["rs0"], 1)

            def round_h(norm):
                for c in range(C):
                    act.wait_ge(norm["h"], c + 1)
                    act.activation(part(h_hi, c), tmp[c % 2][:], ACT.Identity).then_inc(norm["hi"], 1)

            act.wait_ge(const_set, 1)
            act.wait_ge(vec_step, 1)
            act.activation(vec[:, V_S:V_S + C], vec[:, V_S:V_S + C], ACT.Exp, scale=-1.0).then_inc(vec_step, 1)
            for c in range(C):
                act.wait_ge(x_in[c], 16)
                square_chunk(norms[0], x_raw, c)
            inverse_root(norms[0])
            round_weights("A", 0, 0)
            round_weights("A", 0, 1)
            round_h(norms[0])

            def carry_wait(cell):
                act.activation(idle_act[:, cell:cell + 1], ones[:, 0:1], ACT.Identity)

            def layer_a(n, last=False):
                following = ("Y", 0) if last else ("A", n + 1)
                for k in range(2):
                    after(act, conv_done, 2 * n + k)
                    for t, (a, m) in enumerate(ALL_TOKENS):
                        act.wait_ge(a_proj, 24 * n + 3 * k + t + 1)
                        act.activation(u_in[:, 4 + a:4 + a + m], pj[t][:, 0:m], ACT.Identity).then_inc(u_set, 1)
                    round_weights("A", n, 2 + k)
                for k in range(2):
                    act.wait_ge(conv_done, 2 * n + k + 1)
                    act.activation(uc_hi[k][:], u_conv[k][:], ACT.Identity).then_inc(uc_hi_set, 1)
                    for t, (a, m) in enumerate(ALL_TOKENS):
                        act.wait_ge(a_proj, 24 * n + 6 + 3 * k + t + 1)
                        if k == 0:
                            after(act, y_set, 2 * n)
                        else:
                            act.wait_ge(gate_set, 6 * n + t + 1)
                        act.activation(r_buf[:, a:a + m], pj[t][:, 0:m], ACT.Tanh, scale=0.5).then_inc(gate_tanh, 1)
                    round_weights("A", n, 4 + k)
                for k in range(2):
                    ch = 2 * n + k
                    for t, (a, m) in enumerate(ALL_TOKENS):
                        act.wait_ge(a_proj, 24 * n + 12 + 6 * k + t + 1)
                        if k == 0:
                            act.wait_ge(gate_set, 6 * n + 4 + t)
                        else:
                            act.wait_ge(y_set, ch)
                        carry_wait(6 * k + t)
                        act.activation(r_buf[:, a:a + m], pj[t][:, 0:m], ACT.Tanh, scale=0.5,
                                       bias=col(V_B_R, ch)).then_inc(ri_set, 1)
                    act.wait_ge(ri_set, 12 * n + 6 * k + 3)
                    after(act, y_set, ch)
                    act.activation(a_buf[:], r_buf[:], ACT.Exp, scale=col(V_E, ch), bias=col(V_E, ch)).then_inc(a_set, 1)
                    for t, (a, m) in enumerate(ALL_TOKENS):
                        act.wait_ge(a_proj, 24 * n + 15 + 6 * k + t + 1)
                        carry_wait(6 * k + 3 + t)
                        act.activation(i_buf[:, a:a + m], p_i[t][:, 0:m], ACT.Tanh, scale=0.5,
                                       bias=col(V_B_I, ch)).then_inc(ri_set, 1)
                    act.wait_ge(a_set, ch + 1)
                    act.activation(r_buf[:], r_buf[:], ACT.Tanh, scale=col(V_T, ch), bias=col(V_T, ch)).then_inc(t_set, 1)
                    act.wait_ge(t_set, ch + 1)
                    act.activation(r_buf[:], r_buf[:], ACT.Sqrt).then_inc(mult_set, 1)
                    round_weights(*following, k)
                    act.wait_ge(y_set, ch + 1)
                    act.activation(part(y_hi, ch), gate[k][:], ACT.Identity).then_inc(y_hi_set, 1)

            act.wait_ge(pad_set, 1)
            act.wait_ge(vec_step, VEC_STEPS)
            layer_a(0)
            with act.Fori(1, LRU_BLOCKS - 1) as n:
                layer_a(n)
            layer_a(LRU_BLOCKS - 1, last=True)

            def layer_a_out(m, last=False):
                for k in range(2):
                    j = 2 * m + k
                    act.wait_ge(x1_set, 3 * j + 3)
                    square_chunk(norms[1], x1, j)
                    round_weights(*(("B", 0) if last else ("Y", m + 1)), k)

            layer_a_out(0)
            with act.Fori(1, ROUNDS_OUT - 1) as m:
                layer_a_out(m)
            layer_a_out(ROUNDS_OUT - 1, last=True)

            act.wait_ge(wf_scaled, 1)
            act.wait_ge(wf_zero, 2)
            act.activation(wf_hi[:].rearrange("p (c n) -> p c n", c=C)[:, :, 0:HEADS],
                           wf_raw[:].rearrange("p (c n) -> p c n", c=C), ACT.Identity).then_inc(wf_hi_set, 1)
            inverse_root(norms[1])
            round_h(norms[1])
            f = square[0:HEADS, :]
            act.wait_ge(f_in, 3)
            act.activation(f, q_raw[0:HEADS, :], ACT.Abs).then_inc(f_step, 1)
            act.wait_ge(f_step, 1)
            act.activation(f, f, ACT.Exp, scale=-1.0).then_inc(f_step, 1)
            act.wait_ge(f_step, 2)
            act.activation(f, f, ACT.Ln, bias=ones[0:HEADS, 0:1]).then_inc(f_ln, 1)

            def round_probs(h):
                def unit(u):
                    a = UNITS[u][2] * P
                    act.wait_ge(turned, 18 * h + NV + u + 1)
                    if u >= 2:
                        act.wait_ge(pv_done, NU * h + u - 1)
                    act.activation(pt_hi[u % 2][:, a:BANK], pt[u % 2][:, a:BANK], ACT.Identity).then_inc(turned_hi, 1)
                return unit

            def round_values(h, v):
                c0, c1 = V_UNITS[v]
                rows = META if c0 == 0 else P
                act.wait_ge(turned, 18 * h + v + 1)
                act.activation(v_hi[0:rows, c0 * P:c1 * P], pt[v % 2][0:rows, 0:(c1 - c0) * P],
                               ACT.Identity).then_inc(turned_hi, 1)

            def layer_b(h, peeled=False, last=False):
                following = ("O", 0) if last else ("B", h + 1)

                def take(k, raw, tiles, t):
                    a, n = tiles[t]
                    act.wait_ge(b_proj, 12 * h + 3 * k + t + 1)
                    m = act.activation(raw[:, a:a + n], pj[t][:, 0:n], ACT.Identity)
                    if k == 2:
                        m.then_inc(kqv_in, 1)
                        return
                    if k == 1 and t == 0:
                        mean_squares(0)
                    act.activation(square[:, a:a + n], pj[t][:, 0:n], ACT.Square).then_inc(kqv_in, 1)

                def mean_squares(k):
                    for t, (a, n) in enumerate(ALL_TOKENS):
                        act.wait_ge(stat_sum, 6 * h + 3 * k + t + 1)
                        act.activation(ms[:, a:a + n], ps[(t + k) % 2][:, 0:n], ACT.Identity, scale=1.0 / P,
                                       bias=eps[:]).then_inc(ms_set, 1)

                def first_root(k):
                    act.wait_ge(ms_set, 6 * h + 3 * k + 3)
                    act.activation(rs[:], ms[:], ACT.Ln).then_inc(rs0_set, 1)
                    act.wait_ge(rs0_set, 4 * h + 2 * k + 1)
                    act.activation(rs[:], rs[:], ACT.Exp, scale=-0.5).then_inc(rs0_set, 1)

                if peeled:
                    act.wait_ge(f_cum, 1)
                else:
                    act.wait_ge(logits, NP * h)
                    act.wait_ge(gate2_set, 3 * h)
                for t in range(3):
                    take(0, k_raw, ALL_TOKENS, t)
                    if not peeled:
                        for v in VALUES_AT[t]:
                            round_values(h - 1, v)
                round_weights("B", h, 2)
                take(1, q_raw, REAL_TOKENS, 0)
                first_root(0)
                take(1, q_raw, REAL_TOKENS, 1)
                take(1, q_raw, REAL_TOKENS, 2)
                act.wait_ge(kq_scaled, 2 * h + 1)
                act.activation(k_hi[:], k_raw[:], ACT.Identity).then_inc(kq_hi_set, 1)
                round_weights("B", h, 3)
                if peeled:
                    act.wait_ge(ncum_out, 16)
                take(2, v_raw, ALL_TOKENS, 0)
                mean_squares(1)
                first_root(1)
                take(2, v_raw, ALL_TOKENS, 1)
                take(2, v_raw, ALL_TOKENS, 2)

                def round_q():
                    act.wait_ge(kq_scaled, 2 * h + 2)
                    act.activation(q_hi[:, META:T], q_raw[:, META:T], ACT.Identity).then_inc(kq_hi_set, 1)
                    round_weights(*following, 0)

                def gate_tanh_tile(t):
                    a, n = REAL_TOKENS[t]
                    act.wait_ge(b_proj, 12 * h + 10 + t)
                    act.activation(ms[:, a:a + n], pj[t][:, 0:n], ACT.Tanh, scale=0.5).then_inc(gate2_tanh, 1)

                if peeled:
                    round_q()
                else:
                    unit = round_probs(h - 1)
                    for u in range(NU):
                        unit(u)
                        if u == UNIT_WITH_Q:
                            round_q()
                gate_tanh_tile(0)
                for i in range(QB):
                    act.wait_ge(logits, NP * h + LAST_PIECE[i] + 1)
                    row = prob[:, ROW[i]:ROW[i] + WIDTH[i]]
                    act.activation(row, row, ACT.Exp, scale=-1.0, bias=shift[:, LAST_PIECE[i]:LAST_PIECE[i] + 1],
                                   accum_out=total[:, i:i + 1]).then_inc(row_exp, 1)
                    if i == ROW_WITH_TILE_1:
                        gate_tanh_tile(1)
                gate_tanh_tile(2)
                if peeled:
                    act.wait_ge(v_zero, 2)
                else:
                    act.wait_ge(pv_done, NU * h)
                round_weights(*following, 1)

            layer_b(0, peeled=True)
            with act.Fori(1, HEADS - 1) as h:
                layer_b(h)
            layer_b(HEADS - 1, last=True)

            def round_og(c):
                act.wait_ge(og_set, 2 * c + 2)
                act.activation(h_hi[:, c * T:c * T + SEQ], og[:, c * SEQ:(c + 1) * SEQ],
                               ACT.Identity).then_inc(og_hi_set, 1)

            for v in range(NV):
                round_values(HEADS - 1, v)
            unit = round_probs(HEADS - 1)
            for u in range(NU):
                unit(u)
                if u in OG_AT:
                    round_og(OG_AT.index(u))
            round_og(HEADS - 1)

            def layer_b_out(m, last=False):
                for k in range(2):
                    j = 2 * m + k
                    if not last:
                        act.wait_ge(o_proj, 3 * j + 3)
                        round_weights("O", m + 1, k)
                    act.wait_ge(y_added, 3 * j + 3)
                    act.dma_start(out_t[bass.ds(j, 1)].rearrange("a p n -> (a p) n"), y_out[k][:]).then_inc(y_stored[k], 16)

            layer_b_out(0)
            with act.Fori(1, ROUNDS_OUT - 1) as m:
                layer_b_out(m)
            layer_b_out(ROUNDS_OUT - 1, last=True)

        @block.vector
        def _(dve):
            def refine(ms_t, rs_t, sem_, at):
                dve.scalar_tensor_tensor(ms_t, rs_t, -0.5, ms_t, ALU.mult, ALU.mult).then_inc(sem_, 1)
                dve.wait_ge(sem_, at + 1)
                dve.tensor_tensor(ms_t, ms_t, rs_t, ALU.mult).then_inc(sem_, 1)
                dve.wait_ge(sem_, at + 2)
                dve.scalar_tensor_tensor(rs_t, ms_t, 1.5, rs_t, ALU.add, ALU.mult).then_inc(sem_, 1)
                dve.wait_ge(sem_, at + 3)

            def scale_to_h(norm, source):
                dve.wait_ge(norm["rs0"], 2)
                refine(sq[:], acc[:], norm["rs"], 0)

                def remainder(c):
                    dve.wait_ge(norm["hi"], c + 1)
                    a, b = c * T + LO_CUT, (c + 1) * T
                    dve.tensor_tensor(h_lo[:, a:b], tmp[c % 2][:, LO_CUT:T], h_hi[:, a:b].bitcast(F32),
                                      ALU.subtract).then_inc(norm["lo_dve"], 1)

                for c in range(C):
                    if c >= 2:
                        dve.wait_ge(norm["lo_pool"], c - 1)
                        dve.wait_ge(norm["lo_dve"], c - 1)
                    dve.tensor_tensor(tmp[c % 2][:], part(source, c), acc[:], ALU.mult).then_inc(norm["h"], 1)
                    if c >= 1:
                        remainder(c - 1)
                remainder(C - 1)

            y, s, s2, series, tail = (vec[:, V_S + i * C:V_S + (i + 1) * C] for i in range(5))
            steps = [0]

            def step(instruction):
                instruction.then_inc(vec_step, 1)
                steps[0] += 1
                dve.wait_ge(vec_step, steps[0])

            lam = vec[:, V_LAMBDA:V_LAMBDA + C]
            dve.wait_ge(vec_in, 16)
            step(dve.scalar_tensor_tensor(y, lam, -1.0, lam, ALU.mult, ALU.max))
            steps[0] += 1
            dve.wait_ge(vec_step, 2)
            step(dve.tensor_scalar(s, y, 2.0, None, ALU.add))
            step(dve.reciprocal(s, s))
            step(dve.tensor_tensor(s, s, y, ALU.mult))
            step(dve.tensor_tensor(s2, s, s, ALU.mult))
            step(dve.tensor_scalar(series, s2, 1.0 / 17, None, ALU.mult))
            for n in (15, 13, 11, 9, 7, 5, 3):
                step(dve.scalar_tensor_tensor(series, series, 1.0 / n, s2, ALU.add, ALU.mult))
            step(dve.scalar_tensor_tensor(series, series, 1.0, s, ALU.add, ALU.mult))
            step(dve.tensor_scalar(tail, lam, -1.0, 0.0, ALU.mult, ALU.max))
            step(dve.scalar_tensor_tensor(series, series, 2.0, tail, ALU.mult, ALU.add))
            step(dve.tensor_scalar(vec[:, V_T:V_T + C], series, 2.0, None, ALU.mult))
            step(dve.tensor_scalar(vec[:, V_E:V_E + C], series, -4.0, None, ALU.mult))
            both = vec[:, V_B_R:V_B_R + 2 * C]
            step(dve.tensor_scalar(both, both, 0.5, None, ALU.mult))
            step(dve.tensor_tensor(col(V_KQ), col(V_K_NORM), col(V_Q_NORM), ALU.mult))
            step(dve.tensor_scalar(col(V_KQ), col(V_KQ), float(P) ** -0.5, None, ALU.mult))
            assert steps[0] == VEC_STEPS, steps[0]
            dve.memset(u_in[:, 0:4], 0.0).then_inc(pad_set, 1)
            scale_to_h(norms[0], x_raw)

            def layer_a(n, peeled=False):
                for k in range(2):
                    ch = 2 * n + k
                    dve.wait_ge(u_set, 6 * n + 3 * k + 3)
                    after(dve, uc_lo_set, ch - 1)
                    dve.tensor_scalar(u_conv[k][:], u_in[:, 1:1 + T], col(V_CONV_W, TAPS * ch),
                                      col(V_CONV_B, ch), ALU.mult, ALU.add).then_inc(conv_step, 1)
                    for tap in range(1, TAPS):
                        dve.wait_ge(conv_step, 4 * n + 2 * n + 3 * k + tap)
                        m = dve.scalar_tensor_tensor(u_conv[k][:], u_in[:, 1 + tap:1 + tap + T],
                                                     col(V_CONV_W, TAPS * ch + tap), u_conv[k][:], ALU.mult, ALU.add)
                        m.then_inc(conv_step if tap < TAPS - 1 else conv_done, 1)
                for k in range(2):
                    after(dve, y_lo_set, 2 * n - 1 + k)
                    for t, (a, m) in enumerate(ALL_TOKENS):
                        dve.wait_ge(gate_tanh, 6 * n + 3 * k + t + 1)
                        dve.scalar_tensor_tensor(gate[k][:, a:a + m], r_buf[:, a:a + m], 1.0, pj[t][:, 0:m],
                                                 ALU.add, ALU.mult).then_inc(gate_set, 1)
                for k in range(2):
                    ch = 2 * n + k
                    dve.wait_ge(ri_set, 12 * n + 6 * k + 6)
                    dve.scalar_tensor_tensor(i_buf[:], i_buf[:], 1.0, u_conv[k][:], ALU.add, ALU.mult).then_inc(m_step, 1)
                    dve.wait_ge(mult_set, ch + 1)
                    dve.scalar_tensor_tensor(r_buf[:], a_buf[:], 1.0, r_buf[:], ALU.add, ALU.mult).then_inc(m_step, 1)
                    dve.wait_ge(m_step, 4 * ch + 2)
                    dve.scalar_tensor_tensor(i_buf[:], i_buf[:], 0.5, r_buf[:], ALU.mult, ALU.mult).then_inc(m_step, 1)
                    dve.wait_ge(m_step, 4 * ch + 3)
                    dve.tensor_tensor_scan(r_buf[:], a_buf[:], i_buf[:], 0.0, ALU.mult, ALU.add).then_inc(m_step, 1)
                    dve.wait_ge(m_step, 4 * ch + 4)
                    dve.scalar_tensor_tensor(gate[k][:], r_buf[:], 0.5, gate[k][:], ALU.mult, ALU.mult).then_inc(y_set, 1)

            layer_a(0, peeled=True)
            with dve.Fori(1, LRU_BLOCKS) as n:
                layer_a(n)

            def layer_a_out(m):
                for k in range(2):
                    j = 2 * m + k
                    dve.wait_ge(x_back[k], 16 * (m + 1))
                    for t, (a, n) in enumerate(ALL_TOKENS):
                        dve.wait_ge(ao_proj, 3 * j + t + 1)
                        dve.tensor_tensor(x1[:, bass.ds(j * T + a, n)], pj[t][:, 0:n], tmp[k][:, a:a + n],
                                          ALU.add).then_inc(x1_set, 1)

            layer_a_out(0)
            with dve.Fori(1, ROUNDS_OUT) as m:
                layer_a_out(m)
            scale_to_h(norms[1], x1)

            dve.memset(ms[0:HEADS, :], 1.0).then_inc(f_ones, 1)
            for t, (a, n) in enumerate(ALL_TOKENS):
                dve.wait_ge(f_proj, t + 1)
                dve.tensor_scalar(q_raw[0:HEADS, a:a + n], pj[t][0:HEADS, 0:n], col(V_B_F, 0, HEADS), None,
                                  ALU.add).then_inc(f_in, 1)
            dve.wait_ge(f_ln, 1)
            dve.scalar_tensor_tensor(rs[0:HEADS, :], q_raw[0:HEADS, :], 0.0, square[0:HEADS, :],
                                     ALU.min, ALU.subtract).then_inc(f_ls, 1)
            dve.wait_ge(f_ls, 1)
            dve.wait_ge(f_ones, 1)
            dve.tensor_tensor_scan(v_raw[0:HEADS, :], ms[0:HEADS, :], rs[0:HEADS, :], 0.0,
                                   ALU.mult, ALU.subtract).then_inc(f_cum, 1)

            def split_probs(h):
                def unit(u):
                    j, c, b0 = UNITS[u]
                    a = b0 * P
                    dve.wait_ge(turned_hi, 18 * h + NV + u + 1)
                    dve.tensor_tensor(pt_lo[u % 2][:, a:BANK], pt[u % 2][:, a:BANK],
                                      pt_hi[u % 2][:, a:BANK].bitcast(F32), ALU.subtract).then_inc(turned_lo, 1)
                    if u - 1 in TILE_END:
                        og_tile(TILE_END.index(u - 1))
                    if u == NU - 1:
                        og_tile(1)

                def og_tile(j):
                    if j == 0:
                        dve.wait_ge(gate2_set, 3 * h + 3)
                    dve.wait_ge(pv_done, NU * h + TILE_END[j] + 1)
                    dve.scalar_tensor_tensor(og[:, bass.ds(h * SEQ + BANK * j, BANK)], po[:], 0.5,
                                             og[:, bass.ds(h * SEQ + BANK * j, BANK)], ALU.mult,
                                             ALU.mult).then_inc(og_set, 1)
                return unit

            def split_values(h):
                for v, (c0, c1) in enumerate(V_UNITS):
                    rows = META if c0 == 0 else P
                    dve.wait_ge(turned_hi, 18 * h + v + 1)
                    dve.tensor_tensor(v_lo[0:rows, c0 * P:c1 * P], pt[v % 2][0:rows, 0:(c1 - c0) * P],
                                      v_hi[0:rows, c0 * P:c1 * P].bitcast(F32), ALU.subtract).then_inc(turned_lo, 1)

            def layer_b(h, peeled=False):
                def gate_tile(t):
                    a, n = REAL_TOKENS[t]
                    dve.wait_ge(gate2_tanh, 3 * h + t + 1)
                    dve.scalar_tensor_tensor(og[:, bass.ds(h * SEQ + a - META, n)], ms[:, a:a + n], 1.0, pj[t][:, 0:n],
                                             ALU.add, ALU.mult).then_inc(gate2_set, 1)

                if not peeled:
                    split_values(h - 1)
                for k, raw, scale in ((0, k_raw[:], col(V_KQ)), (1, q_raw[:, META:T], 1.0)):
                    dve.wait_ge(rs0_set, 4 * h + 2 * k + 2)
                    refine(ms[:], rs[:], newton, 6 * h + 3 * k)
                    dve.scalar_tensor_tensor(raw, raw, scale, rs[:] if k == 0 else rs[:, META:T],
                                             ALU.mult, ALU.mult).then_inc(kq_scaled, 1)
                if not peeled:
                    unit = split_probs(h - 1)
                    for u in range(NU):
                        unit(u)
                else:
                    dve.wait_ge(x1_out, 16)
                gate_tile(0)
                dve.wait_ge(decay_in, 16 * h + 16)

                def inverse(i):
                    dve.wait_ge(row_exp, QB * h + i + 1)
                    dve.reciprocal(inv_total[:, i:i + 1], total[:, i:i + 1]).then_inc(inv_set, 1)

                for s, (i, a, n, _) in enumerate(PIECES):
                    first = s == FIRST_PIECE[i]
                    dve.wait_ge(scores, NP * h + s + 1)
                    if not first:
                        dve.wait_ge(logits, NP * h + s)
                    dve.memset(idle_dve[:, s:s + 1], 0.0)
                    dve.tensor_tensor_reduce(
                        out=prob[:, ROW[i] + a:ROW[i] + a + n], in0=ps[s % 2][:, 0:n], in1=decay[:, a:a + n],
                        scale=-1.0, scalar=3e38 if first else shift[:, s - 1:s], op0=ALU.add, op1=ALU.min,
                        accum_out=shift[:, s:s + 1]).then_inc(logits, 1)
                    if s == LAST_PIECE[i] and i > 0:
                        inverse(i - 1)
                    if s == LAST_PIECE[ROW_WITH_TILE_1] + 1:
                        gate_tile(1)
                inverse(QB - 1)
                gate_tile(2)

            layer_b(0, peeled=True)
            with dve.Fori(1, HEADS) as h:
                layer_b(h)

            def og_remainder(c):
                dve.wait_ge(og_hi_set, c + 1)
                a, b = c * T + LO_CUT, c * T + SEQ
                dve.tensor_tensor(h_lo[:, a:b], og[:, c * SEQ + LO_CUT:(c + 1) * SEQ], h_hi[:, a:b].bitcast(F32),
                                  ALU.subtract).then_inc(og_lo_dve, 1)

            split_values(HEADS - 1)
            unit = split_probs(HEADS - 1)
            for u in range(NU):
                unit(u)
                if u in OG_AT:
                    og_remainder(OG_AT.index(u))
            og_remainder(HEADS - 1)

            def layer_b_out(m):
                for k in range(2):
                    j = 2 * m + k
                    dve.wait_ge(x1_back[k], 16 * (m + 1))
                    after(dve, y_stored[k], 16 * m)
                    for t, (a, n) in enumerate(REAL_TOKENS):
                        dve.wait_ge(o_proj, 3 * j + t + 1)
                        a -= META
                        dve.tensor_tensor(y_out[k][:, a:a + n], pj[t][:, 0:n], x1_in[k][:, a:a + n],
                                          ALU.add).then_inc(y_added, 1)

            layer_b_out(0)
            with dve.Fori(1, ROUNDS_OUT) as m:
                layer_b_out(m)

        @block.gpsimd
        def _(pool):
            def scale_weights(phase, i, k):
                gain = {"A": V_A_NORM, "B": (V_KV_NORM, V_B_NORM)[k % 2]}[phase]
                w = w_raw[k % 2][:].rearrange("p (c n) -> p c n", c=C)
                pool.wait_ge(w_in[k % 2], weights_in(phase, i, k))
                pool.tensor_tensor(w, w, vec[:, gain:gain + C].unsqueeze(2).to_broadcast([P, C, P]),
                                   ALU.mult).then_inc(w_scaled[phase], 1)

            def rest_of_weights(phase, i, k):
                cols = slice(0, width_of(phase, k))
                pool.wait_ge(w_hi_set, job_of(phase, i, k) + 1)
                pool.tensor_tensor(w_lo[k % 2][:, cols], w_raw[k % 2][:, cols], w_hi[k % 2][:, cols].bitcast(F32),
                                   ALU.subtract).then_inc(w_split, 1)

            def add_squares(norm, c):
                pool.wait_ge(norm["sq"], c + 1)
                after(pool, norm["acc"], c)
                pool.tensor_tensor(acc[:], acc[:], sq[:], ALU.add).then_inc(norm["acc"], 1)

            def rest_of_h(norm):
                for c in range(C):
                    pool.wait_ge(norm["hi"], c + 1)
                    a, b = c * T, c * T + LO_CUT
                    pool.tensor_tensor(h_lo[:, a:b], tmp[c % 2][:, 0:LO_CUT], h_hi[:, a:b].bitcast(F32),
                                       ALU.subtract).then_inc(norm["lo_pool"], 1)

            pool.memset(acc[:], 0.0).then_inc(norms[0]["zero"], 1)
            pool.memset(eps[:], EPS)
            pool.memset(ones[:], 1.0).then_inc(const_set, 1)
            pool.memset(ident[:], 0.0).then_inc(ident_zero, 1)
            pool.memset(causal_bf[:], 0.0).then_inc(ident_zero, 1)
            pool.wait_ge(ident_zero, 2)
            pool.affine_select(out=ident[:], in_=ident[:], compare_op=ALU.not_equal, fill=1.0, base=0,
                               pattern=[[-1, P]], channel_multiplier=1).then_inc(ident_set, 1)
            pool.affine_select(out=causal_bf[:], in_=causal_bf[:], compare_op=ALU.is_ge, fill=MASKED, base=0,
                               pattern=[[-1, P]], channel_multiplier=1).then_inc(ident_set, 1)
            pool.wait_ge(ident_set, 2)
            pool.tensor_copy(ident_bf[:], ident[:]).then_inc(ident_set, 1)
            pool.wait_ge(norms[0]["zero"], 1)
            for c in range(C):
                add_squares(norms[0], c)
            pool.wait_ge(vec_in, 16)
            scale_weights("A", 0, 0)
            rest_of_weights("A", 0, 0)
            scale_weights("A", 0, 1)
            rest_of_weights("A", 0, 1)
            rest_of_h(norms[0])

            def layer_a(n, last=False):
                following = ("Y", 0) if last else ("A", n + 1)
                for k in range(2, 4):
                    scale_weights("A", n, k)
                    rest_of_weights("A", n, k)
                for k in range(2):
                    pool.wait_ge(uc_hi_set, 2 * n + k + 1)
                    pool.tensor_tensor(uc_lo[k][:], u_conv[k][:], uc_hi[k][:].bitcast(F32),
                                       ALU.subtract).then_inc(uc_lo_set, 1)
                    rest_of_weights("A", n, 4 + k)
                for k in range(2):
                    if not last:
                        scale_weights(*following, k)
                    rest_of_weights(*following, k)
                    pool.wait_ge(y_hi_set, 2 * n + k + 1)
                    pool.tensor_tensor(part(y_lo, 2 * n + k), gate[k][:], part(y_hi, 2 * n + k).bitcast(F32),
                                       ALU.subtract).then_inc(y_lo_set, 1)

            layer_a(0)
            with pool.Fori(1, LRU_BLOCKS - 1) as n:
                layer_a(n)
            layer_a(LRU_BLOCKS - 1, last=True)

            pool.wait_ge(y_set, C)
            pool.memset(acc[:], 0.0).then_inc(norms[1]["zero"], 1)
            pool.wait_ge(norms[1]["zero"], 1)
            pool.wait_ge(wf_in, 16)
            wf = wf_raw[:].rearrange("p (c n) -> p c n", c=C)
            pool.tensor_tensor(wf, wf, vec[:, V_KV_NORM:V_KV_NORM + C].unsqueeze(2).to_broadcast([P, C, HEADS]),
                               ALU.mult).then_inc(wf_scaled, 1)

            def layer_a_out(m, last=False):
                for k in range(2):
                    add_squares(norms[1], 2 * m + k)
                    following = ("B", 0) if last else ("Y", m + 1)
                    if last:
                        scale_weights(*following, k)
                    rest_of_weights(*following, k)

            layer_a_out(0)
            with pool.Fori(1, ROUNDS_OUT - 1) as m:
                layer_a_out(m)
            layer_a_out(ROUNDS_OUT - 1, last=True)
            pool.wait_ge(ao_proj, 3 * C)
            for t in (wf_hi, wf_lo):
                pool.memset(t[:].bitcast(F32), 0.0).then_inc(wf_zero, 1)
            for t in (v_hi, v_lo):
                pool.memset(t[:, 0:P].bitcast(F32), 0.0).then_inc(v_zero, 1)
            pool.wait_ge(wf_hi_set, 1)
            strided = [t[:].rearrange("p (c n) -> p c n", c=C)[:, :, 0:HEADS] for t in (wf_hi, wf_lo)]
            pool.tensor_tensor(strided[1], wf, strided[0].bitcast(F32), ALU.subtract).then_inc(wf_lo_set, 1)
            rest_of_h(norms[1])

            def layer_b(h, last=False):
                following = ("O", 0) if last else ("B", h + 1)
                scale_weights("B", h, 2)
                rest_of_weights("B", h, 2)
                scale_weights("B", h, 3)
                pool.wait_ge(kq_hi_set, 2 * h + 1)
                pool.tensor_tensor(k_lo[:], k_raw[:], k_hi[:].bitcast(F32), ALU.subtract).then_inc(kq_lo_set, 1)
                rest_of_weights("B", h, 3)
                if not last:
                    scale_weights(*following, 0)
                pool.wait_ge(kq_hi_set, 2 * h + 2)
                pool.tensor_tensor(q_lo[:, META:T], q_raw[:, META:T], q_hi[:, META:T].bitcast(F32),
                                   ALU.subtract).then_inc(kq_lo_set, 1)
                rest_of_weights(*following, 0)
                if not last:
                    scale_weights(*following, 1)
                for i in range(QB):
                    row = prob[:, ROW[i]:ROW[i] + WIDTH[i]]
                    pool.wait_ge(inv_set, QB * h + i + 1)
                    pool.tensor_tensor(idle_pool[:, i:i + 1], ones[:, 0:1], ones[:, 0:1], ALU.mult)
                    pool.tensor_scalar(row, row, inv_total[:, i:i + 1], 1.0, ALU.mult, ALU.mult).then_inc(row_norm, 1)
                rest_of_weights(*following, 1)

            layer_b(0)
            with pool.Fori(1, HEADS - 1) as h:
                layer_b(h)
            layer_b(HEADS - 1, last=True)
            for c in range(HEADS):
                pool.wait_ge(og_hi_set, c + 1)
                a = c * T
                pool.tensor_tensor(h_lo[:, a:a + LO_CUT], og[:, c * SEQ:c * SEQ + LO_CUT],
                                   h_hi[:, a:a + LO_CUT].bitcast(F32), ALU.subtract).then_inc(og_lo_pool, 1)

            def layer_b_out(m):
                for k in range(2):
                    rest_of_weights("O", m + 1, k)

            layer_b_out(0)
            with pool.Fori(1, ROUNDS_OUT - 1) as m:
                layer_b_out(m)


def kernel(x, meta_tokens, a_norm, a_w_in, a_conv_w, a_conv_b, a_w_r, a_b_r, a_w_i, a_b_i,
           a_lambda, a_w_out, kv_norm, w_kv, b_f, k_norm, b_norm, b_w_in, q_norm, b_w_out):
    import numpy as np
    import concourse.bacc as bacc
    from concourse.bass_utils import run_bass_kernel_spmd

    def chunks(v):
        return np.asarray(v).reshape(C, P).T

    def jobs(w):
        w = np.asarray(w)
        return w.reshape(C, P, -1, P).transpose(2, 1, 0, 3).reshape(-1, P, C * P)

    def column(v):
        out = np.zeros((P, 1), np.float32)
        out[:np.size(v), 0] = np.asarray(v).ravel()
        return out

    x, w_kv = np.asarray(x), np.asarray(w_kv)
    x_t = np.concatenate([np.asarray(meta_tokens), x[0]], 0).T.reshape(C, P, T)
    conv_w = np.asarray(a_conv_w)[0].reshape(TAPS, C, P).transpose(2, 1, 0).reshape(P, C * TAPS)
    vectors = np.concatenate(
        [chunks(a_norm[0]), chunks(kv_norm), chunks(b_norm[0]), conv_w, chunks(a_conv_b[0]), chunks(a_b_r[0]),
         chunks(a_b_i[0]), chunks(a_lambda[0]), column(k_norm), column(q_norm[0]), column(b_f)], 1)
    a_in, b_in = jobs(a_w_in[0]), jobs(b_w_in[0])
    k_in, v_in = jobs(w_kv[:, :D]), jobs(w_kv[:, D:2 * D])
    order_a = [job for n in range(LRU_BLOCKS) for job in (a_in[2 * n], a_in[2 * n + 1], a_in[C + 2 * n], a_in[C + 2 * n + 1])]
    order_b = [job for h in range(HEADS) for job in (k_in[h], b_in[h], v_in[h], b_in[C + h])]
    w_jobs = np.concatenate([np.stack(order_a), jobs(a_w_out[0]), np.stack(order_b), jobs(b_w_out[0])], 0)
    ri = np.stack([np.asarray(a_w_r)[0], np.asarray(a_w_i)[0]], 0).reshape(2, LRU_BLOCKS, 2, P, 2, P)
    w_ri = ri.transpose(1, 4, 3, 0, 2, 5).reshape(2 * LRU_BLOCKS, P, 4 * P)
    w_f = w_kv[:, 2 * D:].reshape(C, P, HEADS).transpose(1, 0, 2).reshape(P, C * HEADS)

    nc = bacc.Bacc("TRN2", target_bir_lowering=False, num_devices=1)
    given = {"x_t": x_t, "vectors": vectors, "w_jobs": w_jobs, "w_ri": w_ri, "w_f": w_f}
    given = {n: np.ascontiguousarray(a) for n, a in given.items()}
    args = [nc.dram_tensor(n, a.shape, F32, kind="ExternalInput").ap() for n, a in given.items()]
    args.append(nc.dram_tensor("out_t", (C, P, SEQ), F32, kind="ExternalOutput").ap())
    args.append(nc.dram_tensor("x1_dram", (P, C, T), F32, kind="Internal").ap())
    args.append(nc.dram_tensor("ncum_dram", (HEADS, T), F32, kind="Internal").ap())
    trunk(nc, *args)
    got = run_bass_kernel_spmd(nc, [given], core_ids=[0]).results[0]["out_t"]
    return got.reshape(D, SEQ).T.reshape(1, SEQ, D)
```

```python
from contextlib import ExitStack

import concourse.bass as bass
from concourse import mybir

F32 = mybir.dt.float32
F32R = mybir.dt.float32r
BF16 = mybir.dt.bfloat16
ALU = mybir.AluOpType
ACT = mybir.ActivationFunctionType

P = 128
D = 1024
C = D // P
META = 16
SEQ = 1024
T = META + SEQ
HEADS = 8
QB = SEQ // P
TAPS = 4
LRU_BLOCKS = 4
EPS = 1e-6
LO_CUT = 400
MASKED = -1e30
BANK = 512
FAST_COLUMNS = 256

ALL_TOKENS = [(0, 346), (346, 346), (692, 348)]
REAL_TOKENS = [(META, 342), (META + 342, 342), (META + 684, 340)]

PER_ROUND = {"A": 6, "Y": 2, "B": 4, "O": 2}
FIRST_JOB = {"A": 0, "Y": 6 * LRU_BLOCKS, "B": 6 * LRU_BLOCKS + C, "O": 6 * LRU_BLOCKS + C + 4 * HEADS}
W_PER_ROUND = {"A": 4, "Y": 2, "B": 4, "O": 2}
W_FIRST = {"A": 0, "Y": 4 * LRU_BLOCKS, "B": 4 * LRU_BLOCKS + C, "O": 4 * LRU_BLOCKS + C + 4 * HEADS}
ROUNDS_OUT = C // 2

V_A_NORM, V_KV_NORM, V_B_NORM = 0, C, 2 * C
V_CONV_W = 3 * C
V_CONV_B = V_CONV_W + TAPS * C
V_B_R, V_B_I, V_LAMBDA = V_CONV_B + C, V_CONV_B + 2 * C, V_CONV_B + 3 * C
V_K_NORM = V_LAMBDA + C
V_Q_NORM = V_K_NORM + 1
V_B_F = V_Q_NORM + 1
V_ALL = V_B_F + 1
V_KQ = V_ALL
V_T = V_KQ + 1
V_E = V_T + C
V_S = V_E + C
V_END = V_S + 5 * C
VEC_STEPS = 22

WIDTH = [META + P * (i + 1) for i in range(QB)]
ROW = [sum(WIDTH[:i]) for i in range(QB)]
ROWS = sum(WIDTH)


def pieces_of(width):
    n = -(-width // BANK)
    step = width // n // 2 * 2
    return [(a * step, step if a < n - 1 else width - step * (n - 1)) for a in range(n)]


PIECES = [(i, a, n, a + n == WIDTH[i]) for i in range(QB) for a, n in pieces_of(WIDTH[i])]
NP = len(PIECES)
LAST_PIECE = [max(s for s, p in enumerate(PIECES) if p[0] == i) for i in range(QB)]
FIRST_PIECE = [min(s for s, p in enumerate(PIECES) if p[0] == i) for i in range(QB)]

UNITS = [(j, c, max(0, c - 1 - 4 * j)) for j in range(2) for c in range(0, 4 * j + 5)]
NU = len(UNITS)
TILE_END = [max(u for u, x in enumerate(UNITS) if x[0] == j) for j in range(2)]
V_UNITS = [(0, 1), (1, 4), (4, 7), (7, 9)]
NV = len(V_UNITS)
VALUES_AT = [(0, 1), (2,), (3,)]
OG_AT = [0, 2, 4, 6, 8]
REFINED_AT, SCALED_AT = [1, 3, 4], 6
UNIT_WITH_Q = 7
UNIT_WITH_WEIGHTS = 8
SUMS_AFTER = 4
OUT_CHUNK_AT = [1, 3, 5, 7, 9, 11]


GATE_STEPS = [(t, c) for t in range(3) for c in range(C)]
RING = 3
STEPS_AT_UNIT = [2, 1, 1, 1, 1, 1, 1, 1, 0, 1, 0, 0, 0, 0]
GATE_IN_UNITS = sum(STEPS_AT_UNIT)
assert GATE_IN_UNITS + NP == len(GATE_STEPS)
TILE_1_PIECE = 2 * C - 1 - GATE_IN_UNITS
ROW_WITH_TILE_1 = min(i for i in range(QB) if LAST_PIECE[i] > TILE_1_PIECE)


def key_at(c):
    return 0 if c == 0 else META + P * (c - 1)


def after(eng, sem, value):
    if isinstance(value, int) and value <= 0:
        return
    eng.wait_ge(sem, value)


def part(tensor, index, size=T):
    return tensor[:, bass.ds(index * size, size)]


def job_of(phase, i, k):
    return FIRST_JOB[phase] + PER_ROUND[phase] * i + k


def trunk(nc, x_t, vectors, w_jobs, w_ri, w_f, out_t, x1_dram, ncum_dram):
    with ExitStack() as ctx:
        def sem(name):
            return ctx.enter_context(nc.semaphore(name))

        base = (nc.sbuf_base + 63) // 64 * 64
        top = [base]

        def put(name, cols, dt=F32, parts=P, at=None):
            size = cols * (2 if dt == BF16 else 4)
            where = top[0] if at is None else at[0]
            t = nc.alloc_sbuf_tensor_at(name, [parts, cols], dt, offset=where)
            (top if at is None else at)[0] = (where + size + 31) // 32 * 32
            return t

        h_hi, h_lo = put("h_hi", C * T, F32R), put("h_lo", C * T, F32R)
        w_raw = [put(f"w_raw{i}", D) for i in range(2)]
        w_hi = [put(f"w_hi{i}", D, F32R) for i in range(2)]
        w_lo = [put(f"w_lo{i}", D, F32R) for i in range(2)]
        vec = put("vec", V_END)
        ident = put("ident", P)
        eps = put("eps", 1)
        idle_act, idle_dve, idle_pool = put("idle_act", 12), put("idle_dve", NP), put("idle_pool", QB)
        ident_bf, causal_bf = put("ident_bf", P, BF16), put("causal_bf", P, BF16)
        ones = put("ones", P)
        wf_raw = put("wf_raw", C * HEADS)
        shift, total, inv_total = put("shift", NP), put("total", QB), put("inv_total", QB)
        region_y = top[0]
        y_hi, y_lo = put("y_hi", C * T, F32R), put("y_lo", C * T, F32R)
        scratch = top[0]

        x_raw = put("x_raw", C * T, at=[region_y])
        at = [scratch]
        u_in = put("u_in", 4 + T, at=at)
        u_conv = [put(f"u_conv{k}", T, at=at) for k in range(2)]
        conv_split = at[0]
        uc_hi = [put(f"uc_hi{k}", T, F32R, at=at) for k in range(2)]
        uc_lo = [put(f"uc_lo{k}", T, F32R, at=at) for k in range(2)]
        gate = [put(f"gate{k}", T, at=at) for k in range(2)]
        r_buf = [put("r_buf0", T, at=at)[:], u_in[:, 4:4 + T]]
        i_buf0, a_buf0 = put("i_buf0", T, at=at), put("a_buf0", T, at=at)
        end = at[0]
        at = [conv_split]
        _, a_buf1, t_buf1, i_buf1 = (put(n, T, at=at) for n in ("u_hi_place", "a_buf1", "t_buf1", "i_buf1"))
        a_buf, t_buf, i_buf = (a_buf0[:], a_buf1[:]), (r_buf[0], t_buf1[:]), (i_buf0[:], i_buf1[:])
        rs_x = put("rs_x", T, at=[region_y + 4 * (2 * C - 1) * T])
        at = [scratch]
        x1 = put("x1", C * T, at=at)
        tmp = [put(f"tmp{i}", T, at=at) for i in range(2)]
        sq, acc = put("sq", T, at=at), put("acc", T, at=at)
        end = max(end, at[0])
        squares_x = [sq, tmp[0]]
        f_val, f_log, f_sum = (t[0:HEADS, :] for t in (tmp[0], tmp[1], sq))
        at = [scratch]
        og = put("og", HEADS * SEQ, at=at)
        prob = put("prob", ROWS, at=at)
        end = max(end, at[0])
        at = [region_y]
        k_hi, k_lo = put("k_hi", T, F32R, at=at), put("k_lo", T, F32R, at=at)
        q_hi, q_lo = put("q_hi", T, F32R, at=at), put("q_lo", T, F32R, at=at)
        v_hi, v_lo = put("v_hi", 9 * P, F32R, at=at), put("v_lo", 9 * P, F32R, at=at)
        k_raw = put("k_raw", T, at=at)
        decay = k_raw
        q_raw, v_raw = put("q_raw", T, at=at), put("v_raw", T, at=at)
        pt_hi = [put(f"pt_hi{i}", BANK, F32R, at=at) for i in range(2)]
        pt_lo = [put(f"pt_lo{i}", BANK, F32R, at=at) for i in range(2)]
        square_place = at[0]
        square = put("square", T, at=at)
        pt_hi.append(put("pt_hi2", BANK, F32R, at=[square_place]))
        pt_lo.append(put("pt_lo2", BANK, F32R, at=[square_place + 4 * BANK]))
        ms = put("ms", T, at=at)
        rs = put("rs", T, at=at)
        rs_x1 = put("rs_x1", T, at=at)
        assert at[0] <= scratch and end <= nc.sbuf_usable_end, (at[0], scratch, end)
        at = [region_y]
        wf_hi, wf_lo = put("wf_hi", C * P, F32R, at=at), put("wf_lo", C * P, F32R, at=at)
        at = [region_y]
        x1_in = [put(f"x1_in{i}", SEQ, at=at) for i in range(2)]
        y_out = [put(f"y_out{i}", SEQ, at=at) for i in range(2)]

        pj = [ctx.enter_context(nc.psum_tensor(f"pj{t}", [P, BANK], F32)) for t in range(3)]
        ps = [ctx.enter_context(nc.psum_tensor(f"ps{t}", [P, BANK], F32)) for t in range(2)]
        pt = [ctx.enter_context(nc.psum_tensor(f"pt{t}", [P, BANK], F32)) for t in range(2)]
        po = ctx.enter_context(nc.psum_tensor("po", [P, BANK], F32))
        p_i = [ps[0], ps[1], pt[0]]
        p_unit = [pt[0], pt[1], ps[0]]
        p_sum = [pt[0], pt[1], pt[0]]
        p_out = [ps[0], ps[1], pt[0]]
        p_extra = [ps[0], ps[1], po]

        def sems(*names):
            return [sem(n) for n in names]

        vec_in, wf_in, x_in, w_in = sem("vec_in"), sem("wf_in"), sems(*(f"x_in{c}" for c in range(C))), sems("w_in0", "w_in1")
        const_set, ident_zero, ident_set, vec_step, wf_scaled, wf_zero, wf_hi_set, wf_lo_set = sems(
            "const_set", "ident_zero", "ident_set", "vec_step", "wf_scaled", "wf_zero", "wf_hi_set", "wf_lo_set")
        w_scaled = {"A": sem("w_scaled_a"), "B": sem("w_scaled_b")}
        w_hi_set, w_split = sems("w_hi_set", "w_split")
        norms = [{k: sem(f"norm{i}_{k}") for k in ("sq", "acc", "sum", "ms", "rs0", "rs", "hi", "lo_pool",
                                                    "lo_dve")} for i in range(2)]
        a_proj, pad_set, u_set, conv_step, conv_done, uc_hi_set, uc_lo_set = sems(
            "a_proj", "pad_set", "u_set", "conv_step", "conv_done", "uc_hi_set", "uc_lo_set")
        gate_raw, gate_tanh, gate_set, ri_set, a_set, t_set, mult_set, m_step, y_set, y_hi_set, y_lo_set = sems(
            "gate_raw", "gate_tanh", "gate_set", "ri_set", "a_set", "t_set", "mult_set", "m_step", "y_set", "y_hi_set",
            "y_lo_set")
        ao_proj, x_back, x1_set, x1_out = sem("ao_proj"), sems("x_back0", "x_back1"), sem("x1_set"), sem("x1_out")
        f_proj, f_raw, f_in, f_step, f_ln, f_ls, f_cum, f_ones, ncum_out = sems(
            "f_proj", "f_raw", "f_in", "f_step", "f_ln", "f_ls", "f_cum", "f_ones", "ncum_out")
        b_proj, kqv_in, squared, stat_sum, ms_set, rs0_set, newton, kq_scaled, kq_hi_set, kq_lo_set = sems(
            "b_proj", "kqv_in", "squared", "stat_sum", "ms_set", "rs0_set", "newton", "kq_scaled", "kq_hi_set", "kq_lo_set")
        decay_in, scores, logits, row_exp, inv_set, row_norm, gate2_raw, gate2_tanh, gate2_set = sems(
            "decay_in", "scores", "logits", "row_exp", "inv_set", "row_norm", "gate2_raw", "gate2_tanh", "gate2_set")
        turned, turned_hi, turned_lo, pv_done, og_set, v_zero = sems(
            "turned", "turned_hi", "turned_lo", "pv_done", "og_set", "v_zero")
        og_hi_set, og_lo_pool, og_lo_dve, o_proj, y_added = sems(
            "og_hi_set", "og_lo_pool", "og_lo_dve", "o_proj", "y_added")
        x1_back, y_stored = sems("x1_back0", "x1_back1"), sems("y_stored0", "y_stored1")

        def col(offset, index=0, parts=P):
            return vec[0:parts, bass.ds(offset + index, 1)]

        def weights_in(phase, i, k):
            return 16 * ((FIRST_JOB[phase] + k) // 2 + PER_ROUND[phase] // 2 * i + 1)

        def width_of(phase, k):
            return 4 * P if phase == "A" and k >= 4 else D

        block = ctx.enter_context(nc.Block())

        @block.sync
        def _(sp):
            def load(phase, i, k):
                after(sp, w_split, job_of(phase, i, k) - 1)
                if phase == "A" and k >= 4:
                    source = w_ri[bass.ds(2 * i + k - 4, 1)]
                else:
                    source = w_jobs[bass.ds(W_FIRST[phase] + W_PER_ROUND[phase] * i + k, 1)]
                sp.dma_start(w_raw[k % 2][:, 0:width_of(phase, k)],
                             source.rearrange("a p n -> (a p) n")).then_inc(w_in[k % 2], 16)

            sp.dma_start(vec[:, 0:V_ALL], vectors).then_inc(vec_in, 16)
            load("A", 0, 0)
            for c in range(C):
                sp.dma_start(part(x_raw, c), x_t[c]).then_inc(x_in[c], 16)
                if c == 2:
                    load("A", 0, 1)
            sp.dma_start(wf_raw[:], w_f).then_inc(wf_in, 16)
            for k in range(2, 6):
                load("A", 0, k)
            with sp.Fori(1, LRU_BLOCKS) as n:
                for k in range(6):
                    load("A", n, k)

            def chunk_again(m, k):
                after(sp, x1_set, 3 * (2 * m + k) - 3)
                sp.dma_start(tmp[k][:], x_t[bass.ds(2 * m + k, 1)].rearrange("a p n -> (a p) n")).then_inc(x_back[k], 16)

            for m in range(2):
                for k in range(2):
                    load("Y", m, k)
            sp.wait_ge(y_lo_set, C)
            chunk_again(0, 0)
            chunk_again(0, 1)
            with sp.Fori(1, ROUNDS_OUT - 1) as m:
                for k in range(2):
                    load("Y", m + 1, k)
                    chunk_again(m, k)
            for k in range(2):
                load("B", 0, k)
                chunk_again(ROUNDS_OUT - 1, k)
            sp.wait_ge(x1_set, 3 * C)
            sp.dma_start(x1_dram, x1[:].rearrange("p (c t) -> p c t", c=C)).then_inc(x1_out, 16)

            def decay_of(h):
                sp.wait_ge(kq_lo_set, 2 * h + 1)
                sp.dma_start(decay[:], ncum_dram[bass.ds(h, 1), :].to_broadcast([P, T])).then_inc(decay_in, 16)

            load("B", 0, 2)
            load("B", 0, 3)
            sp.wait_ge(f_cum, 1)
            sp.dma_start(ncum_dram, f_sum).then_inc(ncum_out, 16)
            sp.wait_ge(ncum_out, 16)
            decay_of(0)
            with sp.Fori(1, HEADS) as h:
                for k in range(4):
                    load("B", h, k)
                decay_of(h)

            def x1_again(m, k):
                after(sp, y_added, 3 * (2 * m + k) - 3)
                sp.dma_start(x1_in[k][:], x1_dram[:, bass.ds(2 * m + k, 1), META:T].rearrange("p a t -> p (a t)")
                             ).then_inc(x1_back[k], 16)

            load("O", 0, 0)
            load("O", 0, 1)
            sp.wait_ge(x1_out, 16)
            sp.wait_ge(scores, NP * HEADS)
            x1_again(0, 0)
            x1_again(0, 1)
            with sp.Fori(1, ROUNDS_OUT) as m:
                for k in range(2):
                    load("O", m, k)
                    x1_again(m, k)
            for k in range(2):
                sp.wait_ge(y_stored[k], 16 * ROUNDS_OUT)

        @block.tensor
        def _(pe):
            def product(out, pairs, start=True, stop=True):
                for i, ((a_hi, a_lo), (b_hi, b_lo)) in enumerate(pairs):
                    pe.matmul(out, a_hi, b_hi, start=(start and i == 0), stop=False)
                    pe.matmul(out, a_hi, b_lo, start=False, stop=False)
                    last = pe.matmul(out, a_lo, b_hi, start=False, stop=(stop and i == len(pairs) - 1))
                return last

            def w_chunk(slot, c):
                return w_hi[slot][:, c * P:(c + 1) * P], w_lo[slot][:, c * P:(c + 1) * P]

            def moving(hi, lo, c, a, n):
                return hi[:, c * T + a:c * T + a + n], lo[:, c * T + a:c * T + a + n]

            def project(slot, t, tiles, hi, lo, shift=0, banks=pj, first=0, end=C):
                a, n = tiles[t]
                return product(banks[t][:, 0:n],
                               [(w_chunk(slot, c), moving(hi, lo, c, a - shift, n)) for c in range(first, end)],
                               start=(first == 0), stop=(end == C))

            def project_as_chunks_come(norm, done, between):
                for c in range(C):
                    pe.wait_ge(norm["lo_pool"], c + 1)
                    pe.wait_ge(norm["lo_dve"], c + 1)
                    for t, (a, n) in enumerate(ALL_TOKENS):
                        (wh, wl), (xh, xl) = w_chunk(0, c), moving(h_hi, h_lo, c, a, n)
                        pe.matmul(pj[t][:, 0:n], wh, xh, start=(c == 0), stop=False)
                        pe.matmul(pj[t][:, 0:n], wh, xl, start=False, stop=False)
                        m = pe.matmul(pj[t][:, 0:n], wl, xh, start=False, stop=(c == C - 1))
                        if c == C - 1:
                            m.then_inc(done, 1)
                    between(c)

            def norm_sums(norm):
                pe.wait_ge(norm["acc"], C - 1)
                for t, (a, n) in enumerate(ALL_TOKENS):
                    if t == 2:
                        pe.wait_ge(norm["ms"], 1)
                    pe.matmul(p_sum[t][:, 0:n], ones[:], acc[:, a:a + n], start=True, stop=True).then_inc(norm["sum"], 1)

            pe.wait_ge(const_set, 1)

            def layer_a(n, peeled=False):
                for k in range(4):
                    pe.wait_ge(w_split, 6 * n + k + 1)
                    if k == 0 and peeled:
                        project_as_chunks_come(norms[0], a_proj, lambda c: None)
                        norm_sums(norms[0])
                        continue
                    for t in range(3):
                        if k == 0:
                            pe.wait_ge(ri_set, 12 * n - 5 + t)
                        elif k == 3:
                            pe.wait_ge(gate_raw, 6 * n + 1 + t)
                        elif k == 2 and peeled:
                            pe.wait_ge(u_set, t + 1)
                        elif not peeled:
                            pe.wait_ge(u_set, 6 * n + 3 * (k - 1) + 1 + t)
                        project(k % 2, t, ALL_TOKENS, h_hi, h_lo, banks=p_extra if peeled and k == 1 else pj
                                ).then_inc(a_proj, 1)
                pe.wait_ge(uc_lo_set, 2 * n + 2)
                for k in range(2):
                    pe.wait_ge(w_split, 6 * n + 5 + k)
                    for g in range(2):
                        for t, (a, m) in enumerate(ALL_TOKENS):
                            if g == 0 and k == 0:
                                pe.wait_ge(gate_raw, 6 * n + 4 + t)
                            elif g == 0:
                                pe.wait_ge(ri_set, 12 * n + 1 + t)
                            else:
                                after(pe, ri_set, 12 * n - 2 + 6 * k + t)
                            product((pj, p_i)[g][t][:, 0:m], [
                                (w_chunk(k, 2 * g + c), (uc_hi[c][:, a:a + m], uc_lo[c][:, a:a + m]))
                                for c in range(2)]).then_inc(a_proj, 1)

            layer_a(0, peeled=True)
            with pe.Fori(1, LRU_BLOCKS) as n:
                layer_a(n)

            def layer_a_out(m):
                for k in range(2):
                    pe.wait_ge(w_split, FIRST_JOB["Y"] + 2 * m + k + 1)
                    for t in range(3):
                        pe.wait_ge(x1_set, 3 * (2 * m + k) - 2 + t)
                        project(k, t, ALL_TOKENS, y_hi, y_lo).then_inc(ao_proj, 1)

            for k in range(2):
                pe.wait_ge(w_split, FIRST_JOB["Y"] + k + 1)
                for t in range(3):
                    if k == 0:
                        pe.wait_ge(ri_set, 12 * LRU_BLOCKS - 5 + t)
                    elif t < 2:
                        pe.wait_ge(ri_set, 12 * LRU_BLOCKS - 2 + t)
                    project(k, t, ALL_TOKENS, y_hi, y_lo, banks=(pj, p_extra)[k], end=C - 2)
            pe.wait_ge(y_lo_set, C)
            for k in range(2):
                for t in range(3):
                    project(k, t, ALL_TOKENS, y_hi, y_lo, banks=(pj, p_extra)[k], first=C - 2).then_inc(ao_proj, 1)
            with pe.Fori(1, ROUNDS_OUT) as m:
                layer_a_out(m)

            def norm_sums_between(c):
                if c == SUMS_AFTER:
                    norm_sums(norms[1])

            def forget_gates():
                pe.wait_ge(wf_lo_set, 1)
                for t, (a, m) in enumerate(ALL_TOKENS):
                    product(p_extra[t][:, 0:m], [
                        ((wf_hi[:, c * P:(c + 1) * P], wf_lo[:, c * P:(c + 1) * P]), moving(h_hi, h_lo, c, a, m))
                        for c in range(C)]).then_inc(f_proj, 1)

            def head_squares(h, which):
                for t, (a, n) in enumerate(ALL_TOKENS):
                    if which == 0 and t == 0:
                        after(pe, logits, NP * h)
                    elif which == 1 or t == 2:
                        pe.wait_ge(ms_set, 6 * h + 3 * which + t - 1)
                    pe.wait_ge(squared, 6 * h + 3 * which + t + 1)
                    pe.matmul(ps[(t + which) % 2][:, 0:n], ones[:], square[:, a:a + n],
                              start=True, stop=True).then_inc(stat_sum, 1)

            def gate_steps(h, first, end):
                for t, c in GATE_STEPS[first:end]:
                    a, n = REAL_TOKENS[t]
                    (wh, wl), (xh, xl) = w_chunk(1, c), moving(h_hi, h_lo, c, a, n)
                    if c == 0:
                        pe.wait_ge(kqv_in, 9 * h + 7 + t)
                    pe.matmul(pj[t][:, 0:n], wh, xh, start=(c == 0), stop=False)
                    pe.matmul(pj[t][:, 0:n], wh, xl, start=False, stop=False)
                    m = pe.matmul(pj[t][:, 0:n], wl, xh, start=False, stop=(c == C - 1))
                    if c == C - 1:
                        m.then_inc(b_proj, 1)

            def probs_times_values(h, between, third_bank_free):
                before = 18 * h + NV
                pe.wait_ge(turned_lo, before)

                def turn(u):
                    j, c, b0 = UNITS[u]
                    if u >= RING:
                        pe.wait_ge(turned_lo, before + u - RING + 1)
                    elif u == RING - 1:
                        pe.wait_ge(*third_bank_free)
                    if c == 0:
                        pe.wait_ge(row_norm, QB * h + 4 * (j + 1))
                    for b in range(b0, 4):
                        at = ROW[4 * j + b] + key_at(c)
                        m = pe.transpose(p_unit[u % RING][:, b * P:(b + 1) * P], prob[:, at:at + P], ident[:])
                    m.then_inc(turned, 1)

                def multiply(u):
                    j, c, b0 = UNITS[u]
                    pe.wait_ge(turned_lo, before + u + 1)
                    if c == 0 and j == 1:
                        pe.wait_ge(og_set, 2 * h + 1)
                    a = b0 * P
                    vh, vl = (v[:, c * P:(c + 1) * P] for v in (v_hi, v_lo))
                    ph, pl = (p[u % RING][:, a:BANK] for p in (pt_hi, pt_lo))
                    pe.matmul(po[:, a:BANK], vh, ph, start=(c == 0), stop=False)
                    pe.matmul(po[:, a:BANK], vh, pl, start=False, stop=False)
                    pe.matmul(po[:, a:BANK], vl, ph, start=False, stop=(u == TILE_END[j])).then_inc(pv_done, 1)

                for u in range(RING - 1):
                    turn(u)
                for u in range(NU):
                    if u + RING - 1 < NU:
                        turn(u + RING - 1)
                    between(u)
                    multiply(u)

            def all_scores(h):
                pe.wait_ge(kq_lo_set, 2 * h + 2)
                for s, (i, a, n, diagonal) in enumerate(PIECES):
                    if s < 2:
                        pe.wait_ge(ms_set, 6 * h + 6)
                    else:
                        pe.wait_ge(logits, NP * h + s - 1)
                    cols = max(n, FAST_COLUMNS)
                    rows, keys = slice(META + P * i, META + P * (i + 1)), slice(a, a + cols)
                    bank = ps[s % 2]
                    pe.matmul(bank[:, 0:cols], q_hi[:, rows], k_hi[:, keys], start=True, stop=False)
                    pe.matmul(bank[:, 0:cols], q_hi[:, rows], k_lo[:, keys], start=False, stop=False)
                    m = pe.matmul(bank[:, 0:cols], q_lo[:, rows], k_hi[:, keys], start=False, stop=not diagonal)
                    if diagonal:
                        m = pe.matmul(bank[:, n - P:n], ident_bf[:], causal_bf[:], start=False, stop=True)
                    m.then_inc(scores, 1)
                    gate_steps(h, GATE_IN_UNITS + s, GATE_IN_UNITS + s + 1)

            def turn_values(h, units):
                for v in units:
                    c0, c1 = V_UNITS[v]
                    if v < 2:
                        pe.wait_ge(kqv_in, 9 * h + 9)
                    else:
                        pe.wait_ge(turned_lo, 18 * h + v - 1)
                    for c in range(c0, c1):
                        m = pe.transpose(pt[v % 2][:, (c - c0) * P:(c - c0 + 1) * P],
                                         v_raw[:, key_at(c):key_at(c) + P], ident[:])
                    m.then_inc(turned, 1)

            def layer_b(h, peeled=False):
                for k, tiles in ((0, ALL_TOKENS), (1, REAL_TOKENS), (2, ALL_TOKENS)):
                    pe.wait_ge(w_split, FIRST_JOB["B"] + 4 * h + k + 1)
                    if k == 0 and peeled:
                        for t in range(3):
                            pe.wait_ge(x1_set, 3 * C - 2 + t)
                        project_as_chunks_come(norms[1], b_proj, norm_sums_between)
                        forget_gates()
                        continue
                    for t in range(3):
                        if k == 0:
                            pe.wait_ge(gate2_raw, 3 * h - 2 + t)
                        else:
                            pe.wait_ge(kqv_in, 9 * h + 3 * (k - 1) + t + 1)
                        project(k % 2, t, tiles, h_hi, h_lo).then_inc(b_proj, 1)
                        if k == 0 and not peeled:
                            turn_values(h - 1, VALUES_AT[t])
                        if k > 0 and t == 0:
                            if peeled and k == 1:
                                pe.wait_ge(f_raw, 3)
                            head_squares(h, k - 1)
                pe.wait_ge(w_split, FIRST_JOB["B"] + 4 * h + 4)
                if peeled:
                    gate_steps(h, 0, GATE_IN_UNITS)
                else:
                    probs_times_values(h - 1, lambda u: gate_steps(
                        h, sum(STEPS_AT_UNIT[:u]), sum(STEPS_AT_UNIT[:u + 1])), (ms_set, 6 * h + 6))
                all_scores(h)

            layer_b(0, peeled=True)
            with pe.Fori(1, HEADS) as h:
                layer_b(h)

            def first_out_chunk(c):
                pe.wait_ge(og_lo_pool, c + 1)
                pe.wait_ge(og_lo_dve, c + 1)
                for t, (a, n) in enumerate(REAL_TOKENS):
                    (wh, wl), (xh, xl) = w_chunk(0, c), moving(h_hi, h_lo, c, a - META, n)
                    pe.matmul(pj[t][:, 0:n], wh, xh, start=(c == 0), stop=False)
                    pe.matmul(pj[t][:, 0:n], wh, xl, start=False, stop=False)
                    m = pe.matmul(pj[t][:, 0:n], wl, xh, start=False, stop=(c == C - 1))
                    if c == C - 1:
                        m.then_inc(o_proj, 1)

            def out_chunks_between(u):
                if u in OUT_CHUNK_AT:
                    first_out_chunk(1 + OUT_CHUNK_AT.index(u))

            turn_values(HEADS - 1, range(NV))
            pe.wait_ge(w_split, FIRST_JOB["O"] + 1)
            pe.wait_ge(gate2_raw, 3 * HEADS)
            first_out_chunk(0)
            probs_times_values(HEADS - 1, out_chunks_between, (logits, NP * HEADS))
            pe.wait_ge(w_split, FIRST_JOB["O"] + 2)
            for t in range(2):
                project(1, t, REAL_TOKENS, h_hi, h_lo, META, banks=p_out, end=C - 1)
            first_out_chunk(HEADS - 1)
            for t in range(3):
                project(1, t, REAL_TOKENS, h_hi, h_lo, META, banks=p_out, first=C - 1 if t < 2 else 0).then_inc(o_proj, 1)

            def layer_b_out(m):
                for k in range(2):
                    pe.wait_ge(w_split, FIRST_JOB["O"] + 2 * m + k + 1)
                    for t in range(3):
                        pe.wait_ge(y_added, 3 * (2 * m + k) - 2 + t)
                        project(k, t, REAL_TOKENS, h_hi, h_lo, META).then_inc(o_proj, 1)

            with pe.Fori(1, ROUNDS_OUT) as m:
                layer_b_out(m)

        @block.scalar
        def _(act):
            def round_weights(phase, i, k):
                if phase in w_scaled and k < 4:
                    act.wait_ge(w_scaled[phase], 4 * i + k + 1)
                else:
                    act.wait_ge(w_in[k % 2], weights_in(phase, i, k))
                cols = slice(0, width_of(phase, k))
                act.activation(w_hi[k % 2][:, cols], w_raw[k % 2][:, cols], ACT.Identity).then_inc(w_hi_set, 1)

            def mean_square(norm):
                for t, (a, n) in enumerate(ALL_TOKENS):
                    act.wait_ge(norm["sum"], t + 1)
                    act.activation(sq[:, a:a + n], p_sum[t][:, 0:n], ACT.Identity, scale=1.0 / D,
                                   bias=eps[:]).then_inc(norm["ms"], 1)

            def inverse_root(norm):
                act.wait_ge(norm["ms"], 3)
                act.activation(acc[:], sq[:], ACT.Ln).then_inc(norm["rs0"], 1)
                act.wait_ge(norm["rs0"], 1)
                act.activation(acc[:], acc[:], ACT.Exp, scale=-0.5).then_inc(norm["rs0"], 1)

            act.wait_ge(const_set, 1)
            act.wait_ge(vec_step, 1)
            act.activation(vec[:, V_S:V_S + C], vec[:, V_S:V_S + C], ACT.Exp, scale=-1.0).then_inc(vec_step, 1)
            for c in range(C):
                if c == 0:
                    round_weights("A", 0, 0)
                act.wait_ge(x_in[c], 16)
                act.activation(part(h_hi, c), part(x_raw, c), ACT.Identity).then_inc(norms[0]["hi"], 1)
                if c == 4:
                    round_weights("A", 0, 1)
                if c >= 3:
                    act.wait_ge(norms[0]["acc"], c - 2)
                act.activation(acc[:] if c == 0 else squares_x[c % 2][:], part(x_raw, c), ACT.Square
                               ).then_inc(norms[0]["sq"], 1)
            mean_square(norms[0])
            inverse_root(norms[0])

            def carry_wait(cell):
                act.activation(idle_act[:, cell:cell + 1], ones[:, 0:1], ACT.Identity)

            def round_y(n, k):
                act.wait_ge(y_set, 2 * n + k + 1)
                act.activation(part(y_hi, 2 * n + k), gate[k][:], ACT.Identity).then_inc(y_hi_set, 1)

            def layer_a(n, peeled=False, last=False):
                following = ("Y", 0) if last else ("A", n + 1)
                for k in range(2):
                    act.wait_ge(a_proj, 24 * n + 3 * k + 3)
                    round_weights("A", n, 2 + k)
                    if k == 0 and not peeled:
                        round_y(n - 1, 1)
                    act.wait_ge(conv_done, 2 * n + k + 1)
                    act.activation(uc_hi[k][:], u_conv[k][:], ACT.Identity).then_inc(uc_hi_set, 1)
                after(act, y_set, 2 * n)
                for k in range(2):
                    act.wait_ge(gate_raw, 6 * n + 3 * k + 3)
                    act.activation(r_buf[k], gate[k][:], ACT.Tanh, scale=0.5).then_inc(gate_tanh, 1)
                    round_weights("A", n, 4 + k)

                def tanh_r(k, ch):
                    for t, (a, m) in enumerate(ALL_TOKENS):
                        act.wait_ge(a_proj, 24 * n + 12 + 6 * k + t + 1)
                        act.wait_ge(gate_set, 2 * n + k + 1)
                        carry_wait(6 * k + t)
                        act.activation(r_buf[k][:, a:a + m], pj[t][:, 0:m], ACT.Tanh, scale=0.5,
                                       bias=col(V_B_R, ch)).then_inc(ri_set, 1)

                def tanh_i(k, ch):
                    for t, (a, m) in enumerate(ALL_TOKENS):
                        act.wait_ge(a_proj, 24 * n + 15 + 6 * k + t + 1)
                        carry_wait(6 * k + 3 + t)
                        act.activation(i_buf[k][:, a:a + m], p_i[t][:, 0:m], ACT.Tanh, scale=0.5,
                                       bias=col(V_B_I, ch)).then_inc(ri_set, 1)

                def decay_and_t(k, ch):
                    act.wait_ge(ri_set, 12 * n + 6 * k + 3)
                    act.activation(a_buf[k], r_buf[k], ACT.Exp, scale=col(V_E, ch), bias=col(V_E, ch)).then_inc(a_set, 1)
                    act.wait_ge(a_set, ch + 1)
                    act.activation(t_buf[k], r_buf[k], ACT.Tanh, scale=col(V_T, ch), bias=col(V_T, ch)).then_inc(t_set, 1)

                tanh_r(0, 2 * n)
                tanh_i(0, 2 * n)
                round_weights(*following, 0)
                tanh_r(1, 2 * n + 1)
                decay_and_t(0, 2 * n)
                tanh_i(1, 2 * n + 1)
                decay_and_t(1, 2 * n + 1)
                if last:
                    round_weights(*following, 1)
                for k in range(2):
                    act.wait_ge(t_set, 2 * n + k + 1)
                    act.activation(t_buf[k], t_buf[k], ACT.Sqrt).then_inc(mult_set, 1)
                if not last:
                    round_weights(*following, 1)
                round_y(n, 0)

            act.wait_ge(vec_step, VEC_STEPS)
            layer_a(0, peeled=True)
            with act.Fori(1, LRU_BLOCKS - 1) as n:
                layer_a(n)
            layer_a(LRU_BLOCKS - 1, last=True)
            round_y(LRU_BLOCKS - 1, 1)

            def layer_a_out(m, last=False):
                for k in range(2):
                    j = 2 * m + k
                    if not last:
                        act.wait_ge(ao_proj, 3 * j + 3)
                        round_weights("Y", m + 1, k)
                    if not (isinstance(j, int) and j < 2):
                        act.wait_ge(norms[1]["acc"], j - 1)
                    act.wait_ge(x1_set, 3 * j + 3)
                    act.activation(part(h_hi, j), part(x1, j), ACT.Identity).then_inc(norms[1]["hi"], 1)
                    act.activation((acc if isinstance(j, int) and j == 0 else sq)[:], part(x1, j), ACT.Square
                                   ).then_inc(norms[1]["sq"], 1)
                    if last:
                        round_weights("B", 0, k)

            layer_a_out(0)
            with act.Fori(1, ROUNDS_OUT - 1) as m:
                layer_a_out(m)
            layer_a_out(ROUNDS_OUT - 1, last=True)

            mean_square(norms[1])
            act.wait_ge(wf_scaled, 1)
            act.wait_ge(wf_zero, 2)
            act.activation(wf_hi[:].rearrange("p (c n) -> p c n", c=C)[:, :, 0:HEADS],
                           wf_raw[:].rearrange("p (c n) -> p c n", c=C), ACT.Identity).then_inc(wf_hi_set, 1)
            inverse_root(norms[1])

            def forget_gates():
                act.wait_ge(f_in, 3)
                act.activation(f_log, f_val, ACT.Abs).then_inc(f_step, 1)
                act.wait_ge(f_step, 1)
                act.activation(f_log, f_log, ACT.Exp, scale=-1.0).then_inc(f_step, 1)
                act.wait_ge(f_step, 2)
                act.activation(f_log, f_log, ACT.Ln, bias=ones[0:HEADS, 0:1]).then_inc(f_ln, 1)

            def round_probs(h):
                def unit(u):
                    a = UNITS[u][2] * P
                    act.wait_ge(turned, 18 * h + NV + u + 1)
                    if u >= RING:
                        act.wait_ge(pv_done, NU * h + u - RING + 1)
                    act.activation(pt_hi[u % RING][:, a:BANK], p_unit[u % RING][:, a:BANK], ACT.Identity).then_inc(turned_hi, 1)
                return unit

            def round_values(h, v):
                c0, c1 = V_UNITS[v]
                rows = META if c0 == 0 else P
                act.wait_ge(turned, 18 * h + v + 1)
                act.activation(v_hi[0:rows, c0 * P:c1 * P], pt[v % 2][0:rows, 0:(c1 - c0) * P],
                               ACT.Identity).then_inc(turned_hi, 1)

            def round_og(c):
                if c == 0:
                    act.wait_ge(b_proj, 12 * HEADS)
                act.wait_ge(og_set, 2 * c + 2)
                act.activation(h_hi[:, c * T:c * T + SEQ], og[:, c * SEQ:(c + 1) * SEQ],
                               ACT.Identity).then_inc(og_hi_set, 1)

            def layer_b(h, peeled=False, last=False):
                following = ("O", 0) if last else ("B", h + 1)

                def square_tile(k, raw, tiles, t):
                    a, n = tiles[t]
                    act.wait_ge(kqv_in, 9 * h + 3 * k + t + 1)
                    act.activation(square[:, a:a + n], raw[:, a:a + n], ACT.Square).then_inc(squared, 1)

                def mean_squares(k):
                    for t, (a, n) in enumerate(ALL_TOKENS):
                        act.wait_ge(stat_sum, 6 * h + 3 * k + t + 1)
                        act.activation(ms[:, a:a + n], ps[(t + k) % 2][:, 0:n], ACT.Identity, scale=1.0 / P,
                                       bias=eps[:]).then_inc(ms_set, 1)

                def first_root(k):
                    act.wait_ge(ms_set, 6 * h + 3 * k + 3)
                    act.activation(rs[:], ms[:], ACT.Ln).then_inc(rs0_set, 1)
                    act.wait_ge(rs0_set, 4 * h + 2 * k + 1)
                    act.activation(rs[:], rs[:], ACT.Exp, scale=-0.5).then_inc(rs0_set, 1)

                for t in range(3):
                    square_tile(0, k_raw, ALL_TOKENS, t)
                    if not peeled:
                        for v in VALUES_AT[t]:
                            round_values(h - 1, v)
                round_weights("B", h, 2)
                if not peeled:
                    act.wait_ge(gate2_set, h)
                mean_squares(0)
                square_tile(1, q_raw, REAL_TOKENS, 0)
                first_root(0)
                square_tile(1, q_raw, REAL_TOKENS, 1)
                square_tile(1, q_raw, REAL_TOKENS, 2)
                round_weights("B", h, 3)
                if peeled:
                    forget_gates()
                act.wait_ge(newton, 6 * h + 3)
                mean_squares(1)
                act.wait_ge(kq_scaled, 2 * h + 1)
                act.activation(k_hi[:], k_raw[:], ACT.Identity).then_inc(kq_hi_set, 1)
                first_root(1)

                def round_q():
                    act.wait_ge(kq_scaled, 2 * h + 2)
                    act.activation(q_hi[:, META:T], q_raw[:, META:T], ACT.Identity).then_inc(kq_hi_set, 1)

                def next_weights():
                    act.wait_ge(b_proj, 12 * h + 9)
                    round_weights(*following, 0)

                if peeled:
                    round_q()
                    next_weights()
                else:
                    unit = round_probs(h - 1)
                    for u in range(NU):
                        unit(u)
                        if u == UNIT_WITH_Q:
                            round_q()
                        elif u == UNIT_WITH_WEIGHTS:
                            next_weights()
                for i in range(QB):
                    act.wait_ge(logits, NP * h + LAST_PIECE[i] + 1)
                    row = prob[:, ROW[i]:ROW[i] + WIDTH[i]]
                    act.activation(row, row, ACT.Exp, scale=-1.0, bias=shift[:, LAST_PIECE[i]:LAST_PIECE[i] + 1],
                                   accum_out=total[:, i:i + 1]).then_inc(row_exp, 1)
                if last:
                    act.wait_ge(pv_done, NU * h)
                    round_values(h, 0)
                    round_values(h, 1)
                    round_og(0)
                    round_values(h, 2)
                    round_values(h, 3)
                act.wait_ge(gate2_raw, 3 * h + 3)
                act.activation(ms[:, META:T], og[:, bass.ds(h * SEQ, SEQ)], ACT.Tanh, scale=0.5).then_inc(gate2_tanh, 1)
                if peeled:
                    act.wait_ge(v_zero, 2)
                elif not last:
                    act.wait_ge(pv_done, NU * h)
                if not last:
                    round_weights(*following, 1)

            layer_b(0, peeled=True)
            with act.Fori(1, HEADS - 1) as h:
                layer_b(h)
            layer_b(HEADS - 1, last=True)

            round_og(1)
            unit = round_probs(HEADS - 1)
            for u in range(NU):
                unit(u)
                if u in OG_AT:
                    round_og(2 + OG_AT.index(u))
                if u == UNIT_WITH_WEIGHTS:
                    round_weights("O", 0, 1)
            round_og(HEADS - 1)

            def layer_b_out(m, last=False):
                for k in range(2):
                    j = 2 * m + k
                    if not last:
                        act.wait_ge(o_proj, 3 * j + 3)
                        round_weights("O", m + 1, k)
                    act.wait_ge(y_added, 3 * j + 3)
                    act.dma_start(out_t[bass.ds(j, 1)].rearrange("a p n -> (a p) n"), y_out[k][:]).then_inc(y_stored[k], 16)

            layer_b_out(0)
            with act.Fori(1, ROUNDS_OUT - 1) as m:
                layer_b_out(m)
            layer_b_out(ROUNDS_OUT - 1, last=True)

        @block.vector
        def _(dve):
            def refine_step(i, ms_t, rs_t, sem_, at, out=None):
                if i > 0:
                    dve.wait_ge(sem_, at + i)
                if i == 0:
                    m = dve.scalar_tensor_tensor(ms_t, rs_t, -0.5, ms_t, ALU.mult, ALU.mult)
                elif i == 1:
                    m = dve.tensor_tensor(ms_t, ms_t, rs_t, ALU.mult)
                else:
                    m = dve.scalar_tensor_tensor(rs_t if out is None else out, ms_t, 1.5, rs_t, ALU.add, ALU.mult)
                m.then_inc(sem_, 1)

            def refine(ms_t, rs_t, sem_, at, out=None):
                for i in range(3):
                    refine_step(i, ms_t, rs_t, sem_, at, out)

            def inverse_rms(norm, out):
                dve.wait_ge(norm["rs0"], 2)
                refine(sq[:], acc[:], norm["rs"], 0, out[:])

            def add_squares(norm, squares, c):
                dve.wait_ge(norm["sq"], c + 1)
                if not (isinstance(c, int) and c < 2):
                    dve.wait_ge(norm["acc"], c - 1)
                dve.tensor_tensor(acc[:], acc[:], squares[:], ALU.add).then_inc(norm["acc"], 1)

            def rest_of_h(norm, source, c):
                dve.wait_ge(norm["hi"], c + 1)
                cols = bass.ds(c * T + LO_CUT, T - LO_CUT)
                dve.tensor_tensor(h_lo[:, cols], source[:, cols], h_hi[:, cols].bitcast(F32),
                                  ALU.subtract).then_inc(norm["lo_dve"], 1)

            y, s, s2, series, tail = (vec[:, V_S + i * C:V_S + (i + 1) * C] for i in range(5))
            steps = [0]

            def step(instruction):
                instruction.then_inc(vec_step, 1)
                steps[0] += 1
                dve.wait_ge(vec_step, steps[0])

            lam = vec[:, V_LAMBDA:V_LAMBDA + C]
            dve.wait_ge(vec_in, 16)
            step(dve.scalar_tensor_tensor(y, lam, -1.0, lam, ALU.mult, ALU.max))
            steps[0] += 1
            dve.wait_ge(vec_step, 2)
            step(dve.tensor_scalar(s, y, 2.0, None, ALU.add))
            step(dve.reciprocal(s, s))
            step(dve.tensor_tensor(s, s, y, ALU.mult))
            step(dve.tensor_tensor(s2, s, s, ALU.mult))
            step(dve.tensor_scalar(series, s2, 1.0 / 17, None, ALU.mult))
            for n in (15, 13, 11, 9, 7, 5, 3):
                step(dve.scalar_tensor_tensor(series, series, 1.0 / n, s2, ALU.add, ALU.mult))
            step(dve.scalar_tensor_tensor(series, series, 1.0, s, ALU.add, ALU.mult))
            step(dve.tensor_scalar(tail, lam, -1.0, 0.0, ALU.mult, ALU.max))
            step(dve.scalar_tensor_tensor(series, series, 2.0, tail, ALU.mult, ALU.add))
            step(dve.tensor_scalar(vec[:, V_T:V_T + C], series, 2.0, None, ALU.mult))
            step(dve.tensor_scalar(vec[:, V_E:V_E + C], series, -4.0, None, ALU.mult))
            both = vec[:, V_B_R:V_B_R + 2 * C]
            step(dve.tensor_scalar(both, both, 0.5, None, ALU.mult))
            step(dve.tensor_tensor(col(V_KQ), col(V_K_NORM), col(V_Q_NORM), ALU.mult))
            step(dve.tensor_scalar(col(V_KQ), col(V_KQ), float(P) ** -0.5, None, ALU.mult))
            assert steps[0] == VEC_STEPS, steps[0]
            dve.memset(u_in[:, 0:4], 0.0).then_inc(pad_set, 1)
            for c in range(C):
                rest_of_h(norms[0], x_raw, c)
                if c > 0:
                    add_squares(norms[0], squares_x[c % 2], c)
            inverse_rms(norms[0], rs_x)
            dve.wait_ge(norms[0]["rs"], 3)
            dve.wait_ge(pad_set, 1)

            def scan(n, k):
                dve.wait_ge(mult_set, 2 * n + k + 1)
                dve.wait_ge(m_step, 8 * n + 2 * k + 2)
                dve.scalar_tensor_tensor(i_buf[k], i_buf[k], 0.5, t_buf[k], ALU.mult, ALU.mult).then_inc(m_step, 1)
                dve.wait_ge(m_step, 8 * n + 2 * k + 5)
                dve.tensor_tensor_scan(t_buf[k], a_buf[k], i_buf[k], 0.0, ALU.mult, ALU.add).then_inc(m_step, 1)
                dve.wait_ge(m_step, 8 * n + 2 * k + 6)
                dve.scalar_tensor_tensor(gate[k][:], t_buf[k], 0.5, gate[k][:], ALU.mult, ALU.mult).then_inc(y_set, 1)

            def layer_a(n, peeled=False):
                def scale(out, banks, first, done):
                    for t, (a, m) in enumerate(ALL_TOKENS):
                        dve.wait_ge(a_proj, first + t + 1)
                        dve.tensor_tensor(out[:, a:a + m], banks[t][:, 0:m], rs_x[:, a:a + m], ALU.mult).then_inc(done, 1)

                for k in range(2):
                    ch = 2 * n + k
                    if k == 1:
                        dve.wait_ge(conv_done, ch)
                    elif not peeled:
                        dve.wait_ge(t_set, ch)
                    scale(u_in[:, 4:4 + T], p_extra if peeled and k == 1 else pj, 24 * n + 3 * k, u_set)
                    if k == 0 and not peeled:
                        scan(n - 1, 1)
                    dve.wait_ge(u_set, 6 * n + 3 * k + 3)
                    after(dve, uc_lo_set, ch - 1)
                    dve.tensor_scalar(u_conv[k][:], u_in[:, 1:1 + T], col(V_CONV_W, TAPS * ch),
                                      col(V_CONV_B, ch), ALU.mult, ALU.add).then_inc(conv_step, 1)
                    for tap in range(1, TAPS):
                        dve.wait_ge(conv_step, 4 * n + 2 * n + 3 * k + tap)
                        m = dve.scalar_tensor_tensor(u_conv[k][:], u_in[:, 1 + tap:1 + tap + T],
                                                     col(V_CONV_W, TAPS * ch + tap), u_conv[k][:], ALU.mult, ALU.add)
                        m.then_inc(conv_step if tap < TAPS - 1 else conv_done, 1)
                for k in range(2):
                    after(dve, y_lo_set, 2 * n - 1 + k)
                    scale(gate[k], pj, 24 * n + 6 + 3 * k, gate_raw)
                    dve.wait_ge(gate_tanh, 2 * n + k + 1)
                    dve.scalar_tensor_tensor(gate[k][:], r_buf[k], 1.0, gate[k][:], ALU.add, ALU.mult).then_inc(gate_set, 1)
                for k in range(2):
                    dve.wait_ge(ri_set, 12 * n + 6 * k + 6)
                    dve.scalar_tensor_tensor(i_buf[k], i_buf[k], 1.0, u_conv[k][:], ALU.add, ALU.mult).then_inc(m_step, 1)
                    dve.wait_ge(a_set, 2 * n + k + 1)
                    dve.wait_ge(m_step, 8 * n + 2 * k + 1)
                    dve.scalar_tensor_tensor(i_buf[k], a_buf[k], 1.0, i_buf[k], ALU.add, ALU.mult).then_inc(m_step, 1)
                scan(n, 0)

            layer_a(0, peeled=True)
            with dve.Fori(1, LRU_BLOCKS) as n:
                layer_a(n)
            scan(LRU_BLOCKS - 1, 1)

            def layer_a_out(m, peeled=False):
                for k in range(2):
                    j = 2 * m + k
                    banks = p_extra if peeled and k == 1 else pj
                    dve.wait_ge(x_back[k], 16 * (m + 1))
                    for t, (a, n) in enumerate(ALL_TOKENS):
                        dve.wait_ge(ao_proj, 3 * j + t + 1)
                        dve.tensor_tensor(x1[:, bass.ds(j * T + a, n)], banks[t][:, 0:n], tmp[k][:, a:a + n],
                                          ALU.add).then_inc(x1_set, 1)
                    rest_of_h(norms[1], x1, j)
                    if not (isinstance(j, int) and j == 0):
                        add_squares(norms[1], sq, j)

            layer_a_out(0, peeled=True)
            with dve.Fori(1, ROUNDS_OUT) as m:
                layer_a_out(m)
            inverse_rms(norms[1], rs_x1)
            dve.wait_ge(norms[1]["rs"], 3)

            def forget_gates_in():
                dve.memset(v_raw[0:HEADS, :], 1.0).then_inc(f_ones, 1)
                for t, (a, n) in enumerate(ALL_TOKENS):
                    dve.wait_ge(f_proj, t + 1)
                    dve.tensor_tensor(f_val[:, a:a + n], p_extra[t][0:HEADS, 0:n], rs_x1[0:HEADS, a:a + n],
                                      ALU.mult).then_inc(f_raw, 1)
                    dve.wait_ge(f_raw, t + 1)
                    dve.tensor_scalar(f_val[:, a:a + n], f_val[:, a:a + n], col(V_B_F, 0, HEADS), None,
                                      ALU.add).then_inc(f_in, 1)

            def forget_gates_summed():
                dve.wait_ge(f_ln, 1)
                dve.scalar_tensor_tensor(f_log, f_val, 0.0, f_log, ALU.min, ALU.subtract).then_inc(f_ls, 1)
                dve.wait_ge(f_ls, 1)
                dve.wait_ge(f_ones, 1)
                dve.tensor_tensor_scan(f_sum, v_raw[0:HEADS, :], f_log, 0.0, ALU.mult, ALU.subtract).then_inc(f_cum, 1)
                dve.wait_ge(f_cum, 1)

            def split_probs(h):
                def unit(u):
                    j, c, b0 = UNITS[u]
                    a = b0 * P
                    dve.wait_ge(turned_hi, 18 * h + NV + u + 1)
                    dve.tensor_tensor(pt_lo[u % RING][:, a:BANK], p_unit[u % RING][:, a:BANK],
                                      pt_hi[u % RING][:, a:BANK].bitcast(F32), ALU.subtract).then_inc(turned_lo, 1)
                    if u - 1 in TILE_END:
                        og_tile(TILE_END.index(u - 1))
                    if u == NU - 1:
                        og_tile(1)

                def og_tile(j):
                    if j == 0:
                        dve.wait_ge(gate2_set, h + 1)
                    dve.wait_ge(pv_done, NU * h + TILE_END[j] + 1)
                    dve.scalar_tensor_tensor(og[:, bass.ds(h * SEQ + BANK * j, BANK)], po[:], 0.5,
                                             og[:, bass.ds(h * SEQ + BANK * j, BANK)], ALU.mult,
                                             ALU.mult).then_inc(og_set, 1)
                return unit

            def split_values(h, units):
                for v in units:
                    c0, c1 = V_UNITS[v]
                    rows = META if c0 == 0 else P
                    dve.wait_ge(turned_hi, 18 * h + v + 1)
                    dve.tensor_tensor(v_lo[0:rows, c0 * P:c1 * P], pt[v % 2][0:rows, 0:(c1 - c0) * P],
                                      v_hi[0:rows, c0 * P:c1 * P].bitcast(F32), ALU.subtract).then_inc(turned_lo, 1)

            def finish_gate(h):
                dve.wait_ge(gate2_tanh, h + 1)
                place = og[:, bass.ds(h * SEQ, SEQ)]
                dve.scalar_tensor_tensor(place, ms[:, META:T], 1.0, place, ALU.add, ALU.mult).then_inc(gate2_set, 1)

            def layer_b(h, peeled=False):
                def take(k, raw, tiles, t):
                    a, n = tiles[t]
                    dve.wait_ge(b_proj, 12 * h + 3 * k + t + 1)
                    dve.tensor_tensor(raw[:, a:a + n], pj[t][:, 0:n], rs_x1[:, a:a + n], ALU.mult).then_inc(kqv_in, 1)

                def gate_tile(t):
                    a, n = REAL_TOKENS[t]
                    dve.wait_ge(b_proj, 12 * h + 9 + t + 1)
                    dve.tensor_tensor(og[:, bass.ds(h * SEQ + a - META, n)], pj[t][:, 0:n], rs_x1[:, a:a + n],
                                      ALU.mult).then_inc(gate2_raw, 1)

                def scale_q():
                    dve.wait_ge(newton, 6 * h + 6)
                    dve.tensor_tensor(q_raw[:, META:T], q_raw[:, META:T], rs[:, META:T], ALU.mult).then_inc(kq_scaled, 1)

                if not peeled:
                    dve.wait_ge(logits, NP * h)
                for t in range(3):
                    take(0, k_raw, ALL_TOKENS, t)
                    if not peeled:
                        split_values(h - 1, VALUES_AT[t])
                        if t == 0:
                            finish_gate(h - 1)
                if peeled:
                    forget_gates_in()
                for t in range(3):
                    take(1, q_raw, REAL_TOKENS, t)
                dve.wait_ge(rs0_set, 4 * h + 2)
                refine(ms[:], rs[:], newton, 6 * h)
                dve.wait_ge(newton, 6 * h + 3)
                dve.scalar_tensor_tensor(k_raw[:], k_raw[:], col(V_KQ), rs[:], ALU.mult, ALU.mult).then_inc(kq_scaled, 1)
                if peeled:
                    forget_gates_summed()
                take(2, v_raw, ALL_TOKENS, 0)
                if peeled:
                    dve.wait_ge(rs0_set, 4)
                    refine(ms[:], rs[:], newton, 3)
                    scale_q()
                take(2, v_raw, ALL_TOKENS, 1)
                take(2, v_raw, ALL_TOKENS, 2)
                if not peeled:
                    unit = split_probs(h - 1)
                    for u in range(NU):
                        unit(u)
                        if u in REFINED_AT:
                            if u == REFINED_AT[0]:
                                dve.wait_ge(rs0_set, 4 * h + 4)
                            refine_step(REFINED_AT.index(u), ms[:], rs[:], newton, 6 * h + 3)
                        elif u == SCALED_AT:
                            scale_q()
                else:
                    dve.wait_ge(x1_out, 16)
                gate_tile(0)
                dve.wait_ge(decay_in, 16 * h + 16)

                def inverse(i):
                    dve.wait_ge(row_exp, QB * h + i + 1)
                    dve.reciprocal(inv_total[:, i:i + 1], total[:, i:i + 1]).then_inc(inv_set, 1)

                for s, (i, a, n, _) in enumerate(PIECES):
                    first = s == FIRST_PIECE[i]
                    dve.wait_ge(scores, NP * h + s + 1)
                    if not first:
                        dve.wait_ge(logits, NP * h + s)
                    dve.memset(idle_dve[:, s:s + 1], 0.0)
                    dve.tensor_tensor_reduce(
                        out=prob[:, ROW[i] + a:ROW[i] + a + n], in0=ps[s % 2][:, 0:n], in1=decay[:, a:a + n],
                        scale=-1.0, scalar=3e38 if first else shift[:, s - 1:s], op0=ALU.add, op1=ALU.min,
                        accum_out=shift[:, s:s + 1]).then_inc(logits, 1)
                    if s == LAST_PIECE[i] and i > 0:
                        inverse(i - 1)
                    if s == LAST_PIECE[ROW_WITH_TILE_1] + 1:
                        gate_tile(1)
                inverse(QB - 1)
                gate_tile(2)

            layer_b(0, peeled=True)
            with dve.Fori(1, HEADS) as h:
                layer_b(h)

            def og_remainder(c):
                dve.wait_ge(og_hi_set, c + 1)
                a, b = c * T + LO_CUT, c * T + SEQ
                dve.tensor_tensor(h_lo[:, a:b], og[:, c * SEQ + LO_CUT:(c + 1) * SEQ], h_hi[:, a:b].bitcast(F32),
                                  ALU.subtract).then_inc(og_lo_dve, 1)

            split_values(HEADS - 1, range(2))
            og_remainder(0)
            split_values(HEADS - 1, range(2, NV))
            og_remainder(1)
            finish_gate(HEADS - 1)
            unit = split_probs(HEADS - 1)
            for u in range(NU):
                unit(u)
                if u in OG_AT:
                    og_remainder(2 + OG_AT.index(u))
            og_remainder(HEADS - 1)

            def layer_b_out(m, peeled=False):
                for k in range(2):
                    j = 2 * m + k
                    banks = p_out if peeled and k == 1 else pj
                    dve.wait_ge(x1_back[k], 16 * (m + 1))
                    after(dve, y_stored[k], 16 * m)
                    for t, (a, n) in enumerate(REAL_TOKENS):
                        dve.wait_ge(o_proj, 3 * j + t + 1)
                        a -= META
                        dve.tensor_tensor(y_out[k][:, a:a + n], banks[t][:, 0:n], x1_in[k][:, a:a + n],
                                          ALU.add).then_inc(y_added, 1)

            layer_b_out(0, peeled=True)
            with dve.Fori(1, ROUNDS_OUT) as m:
                layer_b_out(m)

        @block.gpsimd
        def _(pool):
            def scale_weights(phase, i, k):
                gain = {"A": V_A_NORM, "B": (V_KV_NORM, V_B_NORM)[k % 2]}[phase]
                w = w_raw[k % 2][:].rearrange("p (c n) -> p c n", c=C)
                pool.wait_ge(w_in[k % 2], weights_in(phase, i, k))
                pool.tensor_tensor(w, w, vec[:, gain:gain + C].unsqueeze(2).to_broadcast([P, C, P]),
                                   ALU.mult).then_inc(w_scaled[phase], 1)

            def rest_of_weights(phase, i, k):
                cols = slice(0, width_of(phase, k))
                pool.wait_ge(w_hi_set, job_of(phase, i, k) + 1)
                pool.tensor_tensor(w_lo[k % 2][:, cols], w_raw[k % 2][:, cols], w_hi[k % 2][:, cols].bitcast(F32),
                                   ALU.subtract).then_inc(w_split, 1)

            def rest_of_h(norm, source, c):
                pool.wait_ge(norm["hi"], c + 1)
                cols = bass.ds(c * T, LO_CUT)
                pool.tensor_tensor(h_lo[:, cols], source[:, cols], h_hi[:, cols].bitcast(F32),
                                   ALU.subtract).then_inc(norm["lo_pool"], 1)

            pool.memset(eps[:], EPS)
            pool.memset(ones[:], 1.0).then_inc(const_set, 1)
            pool.memset(ident[:], 0.0).then_inc(ident_zero, 1)
            pool.memset(causal_bf[:], 0.0).then_inc(ident_zero, 1)
            pool.wait_ge(ident_zero, 2)
            pool.affine_select(out=ident[:], in_=ident[:], compare_op=ALU.not_equal, fill=1.0, base=0,
                               pattern=[[-1, P]], channel_multiplier=1).then_inc(ident_set, 1)
            pool.affine_select(out=causal_bf[:], in_=causal_bf[:], compare_op=ALU.is_ge, fill=MASKED, base=0,
                               pattern=[[-1, P]], channel_multiplier=1).then_inc(ident_set, 1)
            pool.wait_ge(ident_set, 2)
            pool.tensor_copy(ident_bf[:], ident[:]).then_inc(ident_set, 1)
            pool.wait_ge(vec_in, 16)
            scale_weights("A", 0, 0)
            rest_of_weights("A", 0, 0)
            for c in range(C):
                rest_of_h(norms[0], x_raw, c)
                if c == 2:
                    scale_weights("A", 0, 1)
                elif c == 5:
                    rest_of_weights("A", 0, 1)

            def rest_of_y(n, k):
                pool.wait_ge(y_hi_set, 2 * n + k + 1)
                pool.tensor_tensor(part(y_lo, 2 * n + k), gate[k][:], part(y_hi, 2 * n + k).bitcast(F32),
                                   ALU.subtract).then_inc(y_lo_set, 1)

            def layer_a(n, peeled=False, last=False):
                following = ("Y", 0) if last else ("A", n + 1)
                for k in range(2, 4):
                    scale_weights("A", n, k)
                    rest_of_weights("A", n, k)
                    if k == 2 and not peeled:
                        rest_of_y(n - 1, 1)
                for k in range(2):
                    pool.wait_ge(uc_hi_set, 2 * n + k + 1)
                    pool.tensor_tensor(uc_lo[k][:], u_conv[k][:], uc_hi[k][:].bitcast(F32),
                                       ALU.subtract).then_inc(uc_lo_set, 1)
                    rest_of_weights("A", n, 4 + k)
                for k in range(2):
                    if not last:
                        scale_weights(*following, k)
                    rest_of_weights(*following, k)
                rest_of_y(n, 0)

            layer_a(0, peeled=True)
            with pool.Fori(1, LRU_BLOCKS - 1) as n:
                layer_a(n)
            layer_a(LRU_BLOCKS - 1, last=True)
            rest_of_y(LRU_BLOCKS - 1, 1)

            pool.wait_ge(wf_in, 16)
            wf = wf_raw[:].rearrange("p (c n) -> p c n", c=C)
            pool.tensor_tensor(wf, wf, vec[:, V_KV_NORM:V_KV_NORM + C].unsqueeze(2).to_broadcast([P, C, HEADS]),
                               ALU.mult).then_inc(wf_scaled, 1)

            def layer_a_out(m, last=False):
                for k in range(2):
                    if not last:
                        rest_of_weights("Y", m + 1, k)
                    rest_of_h(norms[1], x1, 2 * m + k)
                    if last:
                        scale_weights("B", 0, k)
                        rest_of_weights("B", 0, k)

            layer_a_out(0)
            with pool.Fori(1, ROUNDS_OUT - 1) as m:
                layer_a_out(m)
            layer_a_out(ROUNDS_OUT - 1, last=True)
            pool.wait_ge(ao_proj, 3 * C)
            for t in (wf_hi, wf_lo):
                pool.memset(t[:].bitcast(F32), 0.0).then_inc(wf_zero, 1)
            for t in (v_hi, v_lo):
                pool.memset(t[:, 0:P].bitcast(F32), 0.0).then_inc(v_zero, 1)
            pool.wait_ge(wf_hi_set, 1)
            strided = [t[:].rearrange("p (c n) -> p c n", c=C)[:, :, 0:HEADS] for t in (wf_hi, wf_lo)]
            pool.tensor_tensor(strided[1], wf, strided[0].bitcast(F32), ALU.subtract).then_inc(wf_lo_set, 1)

            def layer_b(h, last=False):
                following = ("O", 0) if last else ("B", h + 1)
                scale_weights("B", h, 2)
                rest_of_weights("B", h, 2)
                scale_weights("B", h, 3)
                pool.wait_ge(kq_hi_set, 2 * h + 1)
                pool.tensor_tensor(k_lo[:], k_raw[:], k_hi[:].bitcast(F32), ALU.subtract).then_inc(kq_lo_set, 1)
                rest_of_weights("B", h, 3)
                if not last:
                    scale_weights(*following, 0)
                pool.wait_ge(kq_hi_set, 2 * h + 2)
                pool.tensor_tensor(q_lo[:, META:T], q_raw[:, META:T], q_hi[:, META:T].bitcast(F32),
                                   ALU.subtract).then_inc(kq_lo_set, 1)
                rest_of_weights(*following, 0)
                if not last:
                    scale_weights(*following, 1)
                for i in range(QB):
                    row = prob[:, ROW[i]:ROW[i] + WIDTH[i]]
                    pool.wait_ge(inv_set, QB * h + i + 1)
                    pool.tensor_tensor(idle_pool[:, i:i + 1], ones[:, 0:1], ones[:, 0:1], ALU.mult)
                    pool.tensor_scalar(row, row, inv_total[:, i:i + 1], 1.0, ALU.mult, ALU.mult).then_inc(row_norm, 1)
                if not last:
                    rest_of_weights(*following, 1)

            layer_b(0)
            with pool.Fori(1, HEADS - 1) as h:
                layer_b(h)
            layer_b(HEADS - 1, last=True)
            for c in range(HEADS):
                pool.wait_ge(og_hi_set, c + 1)
                a = c * T
                pool.tensor_tensor(h_lo[:, a:a + LO_CUT], og[:, c * SEQ:c * SEQ + LO_CUT],
                                   h_hi[:, a:a + LO_CUT].bitcast(F32), ALU.subtract).then_inc(og_lo_pool, 1)
                if c == HEADS - 2:
                    rest_of_weights("O", 0, 1)

            def layer_b_out(m):
                for k in range(2):
                    rest_of_weights("O", m + 1, k)

            layer_b_out(0)
            with pool.Fori(1, ROUNDS_OUT - 1) as m:
                layer_b_out(m)


def kernel(x, meta_tokens, a_norm, a_w_in, a_conv_w, a_conv_b, a_w_r, a_b_r, a_w_i, a_b_i,
           a_lambda, a_w_out, kv_norm, w_kv, b_f, k_norm, b_norm, b_w_in, q_norm, b_w_out):
    import numpy as np
    import concourse.bacc as bacc
    from concourse.bass_utils import run_bass_kernel_spmd

    def chunks(v):
        return np.asarray(v).reshape(C, P).T

    def jobs(w):
        w = np.asarray(w)
        return w.reshape(C, P, -1, P).transpose(2, 1, 0, 3).reshape(-1, P, C * P)

    def column(v):
        out = np.zeros((P, 1), np.float32)
        out[:np.size(v), 0] = np.asarray(v).ravel()
        return out

    x, w_kv = np.asarray(x), np.asarray(w_kv)
    x_t = np.concatenate([np.asarray(meta_tokens), x[0]], 0).T.reshape(C, P, T)
    conv_w = np.asarray(a_conv_w)[0].reshape(TAPS, C, P).transpose(2, 1, 0).reshape(P, C * TAPS)
    vectors = np.concatenate(
        [chunks(a_norm[0]), chunks(kv_norm), chunks(b_norm[0]), conv_w, chunks(a_conv_b[0]), chunks(a_b_r[0]),
         chunks(a_b_i[0]), chunks(a_lambda[0]), column(k_norm), column(q_norm[0]), column(b_f)], 1)
    a_in, b_in = jobs(a_w_in[0]), jobs(b_w_in[0])
    k_in, v_in = jobs(w_kv[:, :D]), jobs(w_kv[:, D:2 * D])
    order_a = [job for n in range(LRU_BLOCKS) for job in (a_in[2 * n], a_in[2 * n + 1], a_in[C + 2 * n], a_in[C + 2 * n + 1])]
    order_b = [job for h in range(HEADS) for job in (k_in[h], b_in[h], v_in[h], b_in[C + h])]
    w_jobs = np.concatenate([np.stack(order_a), jobs(a_w_out[0]), np.stack(order_b), jobs(b_w_out[0])], 0)
    ri = np.stack([np.asarray(a_w_r)[0], np.asarray(a_w_i)[0]], 0).reshape(2, LRU_BLOCKS, 2, P, 2, P)
    w_ri = ri.transpose(1, 4, 3, 0, 2, 5).reshape(2 * LRU_BLOCKS, P, 4 * P)
    w_f = w_kv[:, 2 * D:].reshape(C, P, HEADS).transpose(1, 0, 2).reshape(P, C * HEADS)

    nc = bacc.Bacc("TRN2", target_bir_lowering=False, num_devices=1)
    given = {"x_t": x_t, "vectors": vectors, "w_jobs": w_jobs, "w_ri": w_ri, "w_f": w_f}
    given = {n: np.ascontiguousarray(a) for n, a in given.items()}
    args = [nc.dram_tensor(n, a.shape, F32, kind="ExternalInput").ap() for n, a in given.items()]
    args.append(nc.dram_tensor("out_t", (C, P, SEQ), F32, kind="ExternalOutput").ap())
    args.append(nc.dram_tensor("x1_dram", (P, C, T), F32, kind="Internal").ap())
    args.append(nc.dram_tensor("ncum_dram", (HEADS, T), F32, kind="Internal").ap())
    trunk(nc, *args)
    got = run_bass_kernel_spmd(nc, [given], core_ids=[0]).results[0]["out_t"]
    return got.reshape(D, SEQ).T.reshape(1, SEQ, D)
```
